# Optimizing a Trainium2 kernel written in Bass

```python
import math
import jax, jax.numpy as jnp
from jax import lax
import numpy as np

D_MODEL = 1024
BATCH = 1
SEQ = 2048
DEPTH = 1

D_MIX = D_MODEL
CONV_WIDTH = D_MIX // 2
ATTN_WIDTH = D_MIX - CONV_WIDTH
HEAD_DIM = 64
N_ATTN_HEADS = ATTN_WIDTH // HEAD_DIM
CONV_K = 3
Q_BLOCK = 128
LN_EPS = 1e-5
DEEPNORM_ALPHA = (2.0 * DEPTH) ** 0.25
DEEPNORM_BETA = (8.0 * DEPTH) ** -0.25
PROJ_WIDTH = 4 * CONV_WIDTH + 4 * ATTN_WIDTH

kernel_name = "hymba_shortconv_stickbreaking_deepnorm"

def _layer_norm(y, gain, bias):
    y32 = y.astype(jnp.float32)
    mu = jnp.mean(y32, axis=-1, keepdims=True)
    var = jnp.mean(jnp.square(y32 - mu), axis=-1, keepdims=True)
    out = (y32 - mu) * lax.rsqrt(var + LN_EPS) * gain.astype(jnp.float32) + bias.astype(jnp.float32)
    return out.astype(y.dtype)

def _short_conv(b_gate, c_gate, h, conv_w):
    u = c_gate * h
    seq = u.shape[1]
    u_pad = jnp.pad(u, ((0, 0), (CONV_K - 1, 0), (0, 0)))
    y = conv_w[CONV_K - 1] * u_pad[:, CONV_K - 1:CONV_K - 1 + seq]
    for tap in range(CONV_K - 1):
        y = y + conv_w[tap] * u_pad[:, tap:tap + seq]
    return b_gate * y

def _stick_breaking_attention(q, k, v):
    bsz, seq, _ = q.shape
    out_dtype = v.dtype
    def heads(t):
        return t.reshape(bsz, seq, N_ATTN_HEADS, HEAD_DIM).transpose(0, 2, 1, 3).astype(jnp.float32)
    qh = heads(q) * (HEAD_DIM ** -0.5)
    kh, vh = heads(k), heads(v)
    n_blocks = seq // Q_BLOCK
    outs = []
    for blk in range(n_blocks):
        q0 = blk * Q_BLOCK
        kv_len = q0 + Q_BLOCK
        qb = qh[:, :, q0:kv_len]
        kb = kh[:, :, :kv_len]
        vb = vh[:, :, :kv_len]
        z = jnp.einsum('bhqd,bhkd->bhqk', qb, kb)
        t_pos = q0 + jnp.arange(Q_BLOCK)[:, None]
        s_pos = jnp.arange(kv_len)[None, :]
        strict = s_pos < t_pos
        neg_log_keep = jnp.where(strict, jax.nn.softplus(z), 0.0)
        after = lax.cumsum(neg_log_keep, axis=3, reverse=True) - neg_log_keep
        log_w = jax.nn.log_sigmoid(z) - after
        w = jnp.where(strict, jnp.exp(log_w), 0.0)
        outs.append(jnp.einsum('bhqk,bhkd->bhqd', w, vb))
    o = jnp.concatenate(outs, axis=2)
    return o.transpose(0, 2, 1, 3).reshape(bsz, seq, ATTN_WIDTH).astype(out_dtype)

def setup_inputs(seed: int = 0) -> dict:
    key = jax.random.key(seed)
    k_x, k_in, k_conv, k_out, k_g, k_b = jax.random.split(key, 6)
    x = jax.random.normal(k_x, (BATCH, SEQ, D_MODEL), jnp.float32)
    w_in = jax.random.normal(k_in, (DEPTH, D_MODEL, PROJ_WIDTH), jnp.float32) * (D_MODEL ** -0.5)
    conv_w = jax.random.normal(k_conv, (DEPTH, CONV_K, CONV_WIDTH), jnp.float32) * (CONV_K ** -0.5)
    w_out = jax.random.normal(k_out, (DEPTH, D_MIX, D_MODEL), jnp.float32) * (D_MIX ** -0.5) * DEEPNORM_BETA
    ln_gain = 1.0 + 0.05 * jax.random.normal(k_g, (DEPTH, D_MODEL), jnp.float32)
    ln_bias = 0.02 * jax.random.normal(k_b, (DEPTH, D_MODEL), jnp.float32)
    return {"x": x, "w_in": w_in, "conv_w": conv_w, "w_out": w_out,
            "ln_gain": ln_gain, "ln_bias": ln_bias}

def reference(x, w_in, conv_w, w_out, ln_gain, ln_bias):
    h_res = x
    for layer in range(DEPTH):
        proj = jnp.einsum('bsd,de->bse', h_res, w_in[layer])
        b_c, c_c, h_c, z_c, q, k, v, z_a = jnp.split(proj, 8, axis=-1)
        conv_out = jax.nn.silu(z_c) * _short_conv(b_c, c_c, h_c, conv_w[layer])
        attn_out = jax.nn.silu(z_a) * _stick_breaking_attention(q, k, v)
        mix = jnp.concatenate([conv_out, attn_out], axis=-1)
        sub = jnp.einsum('bse,ed->bsd', mix, w_out[layer])
        h_res = _layer_norm(DEEPNORM_ALPHA * h_res + sub, ln_gain[layer], ln_bias[layer])
    return h_res


_drawn_inputs = setup_inputs


def setup_inputs(seed=0):
    import zlib

    import numpy as np

    out = dict(_drawn_inputs(seed))
    spreads = {}
    factors = {'ln_bias': 2.702}
    for name, (base, spread) in spreads.items():
        noise = np.random.default_rng([zlib.crc32(name.encode()), seed]).standard_normal(out[name].shape)
        drawn = base * np.exp(spread * noise) if base else spread * noise
        out[name] = __import__('jax').numpy.asarray(drawn.astype(out[name].dtype))
    for name, factor in factors.items():
        out[name] = (out[name] * factor).astype(out[name].dtype)
    return out
```

```python
import math

import concourse.bass as bass
from concourse import mybir
from contextlib import ExitStack

F32 = mybir.dt.float32
F16 = mybir.dt.float16
ALU = mybir.AluOpType
ACT = mybir.ActivationFunctionType

SEQ, D_MODEL, PROJ = 2048, 1024, 4096
CONV_W = ATTN_W = 512
HEAD_DIM = 64
CONV_K = 3
LN_EPS = 1e-5
ALPHA = 2.0 ** 0.25
PART = 128
DCH = D_MODEL // PART
QT = 512
NQT = SEQ // QT
SUB = QT // PART
NTB = SEQ // PART
PAIRS = ATTN_W // PART
CUT = 60000.0
ROOT = 8.0
X_SCALE, W_SCALE, P_SCALE = 16.0, 512.0, 1024.0
PROJ_SCALE = 1.0 / (X_SCALE * W_SCALE)
EXP_CLAMP = 40.0
TABLES = "natural_log_exp_and_others"

G_B, G_C, G_H, G_ZC, G_Q, G_K, G_V, G_ZA = range(8)


def blocks_of_pair():
    out = []
    for t in reversed(range(NQT)):
        for b in reversed(range(SUB * (t + 1))):
            out.append((t, b, PART * max(0, b - SUB * t)))
    return out


BLOCKS = blocks_of_pair()
NB = len(BLOCKS)
SUMS_BEFORE = [sum(1 for _, b, _ in BLOCKS[:n] if b > 0) for n in range(NB + 1)]
SUMS = SUMS_BEFORE[NB]
TILE_END = {n: t for n, (t, b, _) in enumerate(BLOCKS) if b == 0}

UNITS_IN = [(G_Q, 0, 0), (G_K, 0, 1), (G_V, 0, 2)]
UNITS_IN += [(G_ZA, t, 3) for t in range(NQT)]
for _g, _s in ((G_C, 0), (G_H, 1), (G_B, 2), (G_ZC, 3)):
    UNITS_IN += [(_g, t, _s) for t in range(NQT)]
UNITS_NEXT = [(g, t, s) for t in (3, 2, 1) for g, s in ((G_Q, 0), (G_K, 1), (G_V, 2))]
UNITS_FIRST = UNITS_NEXT
N_FIRST, N_UNITS = len(UNITS_FIRST), len(UNITS_IN) + len(UNITS_NEXT)
PIECES = 3
LAST_UNIT_ZA, LAST_UNIT_ZC = 6, 22


def schedule(last):
    units = UNITS_IN + ([] if last else UNITS_NEXT)
    pieces = [(u, i) for u in range(len(units)) for i in range(PIECES)]
    cols = [QT - c0 + 90 for _, _, c0 in BLOCKS]
    total, done, at = sum(cols), 0, 0
    share = 0.9 if last else 1.0
    steps = []
    for n in range(NB + 1):
        done += cols[n] if n < NB else 0
        want = len(pieces) if n == NB else min(len(pieces), round(len(pieces) * done / (total * share)))
        mine = []
        while at < want:
            u, _ = pieces[at]
            if u >= len(UNITS_IN):
                tile = units[u][1]
                end = max(m for m, t in TILE_END.items() if t == tile)
                if n < end + 2:
                    break
            mine.append(pieces[at])
            at += 1
        steps.append(mine)
    assert at == len(pieces)
    return units, steps


def layer_program(nc, x, x_blocks, w_blocks, conv_taps_in, w_out, ln_gain, ln_bias, out):
    mix_hi = nc.dram_tensor("mix_hi", [2 * PAIRS, PART, SEQ], F16, kind="Internal").ap()
    mix_lo = nc.dram_tensor("mix_lo", [2 * PAIRS, PART, SEQ], F16, kind="Internal").ap()
    x_rows = x[0].rearrange("(i p) d -> i p d", p=PART)
    out_rows = out[0].rearrange("(i p) d -> i p d", p=PART)
    wo_rows = w_out[0].rearrange("(c p) n -> c p n", p=PART)

    with ExitStack() as ctx:
        def sb(name, shape, dt):
            return ctx.enter_context(nc.sbuf_tensor(name, shape, dt))

        def sem(name):
            return ctx.enter_context(nc.semaphore(name))

        xt_hi = sb("xt_hi", [PART, DCH, SEQ], F16)
        xt_lo = sb("xt_lo", [PART, DCH, SEQ], F16)
        w_raw = sb("w_raw", [PART, 2, DCH, PART], F32)
        w_hi = sb("w_hi", [PART, 4, DCH, PART], F16)
        w_lo = sb("w_lo", [PART, 4, DCH, PART], F16)
        q_hi = sb("q_hi", [PART, SEQ], F16)
        q_lo = sb("q_lo", [PART, SEQ], F16)
        k_hi = sb("k_hi", [PART, SEQ], F16)
        k_lo = sb("k_lo", [PART, SEQ], F16)
        v_hi = sb("v_hi", [PART, NTB, PART], F16)
        v_lo = sb("v_lo", [PART, NTB, PART], F16)
        sp = sb("sp", [PART, 2, 2, QT], F32)
        sp_hi = sb("sp_hi", [PART, 2, QT], F16)
        sp_lo = sb("sp_lo", [PART, 2, QT], F16)
        wt = sb("wt", [PART, 2, QT], F32)
        wt_hi = sb("wt_hi", [PART, 2, 2, QT], F16)
        wt_lo = sb("wt_lo", [PART, 2, 2, QT], F16)
        carry_hi = sb("carry_hi", [PART, QT], F16)
        carry = sb("carry", [PART, QT], F16)
        u_conv = sb("u_conv", [PART, CONV_K - 1 + SEQ], F32)
        b_gate = sb("b_gate", [PART, SEQ], F32)
        z_conv = sb("z_conv", [PART, SEQ], F32)
        z_attn = sb("z_attn", [PART, SEQ], F32)
        y_conv = sb("y_conv", [PART, QT], F32)
        cm_hi = sb("cm_hi", [PART, QT], F16)
        cm_lo = sb("cm_lo", [PART, QT], F16)
        o_gated = sb("o_gated", [PART, QT], F32)
        om_hi = sb("om_hi", [PART, QT], F16)
        om_lo = sb("om_lo", [PART, QT], F16)
        tri = sb("tri", [PART, PART], F16)
        future = sb("future", [PART, PART], F16)
        root_id = sb("root_id", [PART, PART], F16)
        ones = sb("ones", [PART, HEAD_DIM], F16)
        spread = sb("spread", [PART, PART], F16)
        low_rows = sb("low_rows", [PART, 1], F32)
        p_bias = sb("p_bias", [PART, 1], F32)
        eps = sb("eps", [PART, 1], F32)
        w_scale = sb("w_scale", [PART, 1], F32)
        taps = sb("taps", [PART, PAIRS, CONV_K], F32)
        given = sb("given", [PART, 8], F32)
        stats = sb("stats", [PART, 2, 12], F32)
        mean_var = sb("mean_var", [PART, 2, 2], F32)
        log_var = sb("log_var", [PART, 2], F32)
        rstd = sb("rstd", [PART, 2], F32)

        arg = [ctx.enter_context(nc.psum_tensor(f"arg{i}", [PART, 2, QT], F32)) for i in range(2)]
        sums = ctx.enter_context(nc.psum_tensor("sums", [PART, QT], F32))
        o_acc = ctx.enter_context(nc.psum_tensor("o_acc", [PART, QT], F32))
        proj = [ctx.enter_context(nc.psum_tensor(f"proj{i}", [PART, QT], F32)) for i in range(2)]

        x_in = [buf[:, h * D_MODEL:(h + 1) * D_MODEL] for buf in (b_gate, z_conv, z_attn) for h in range(2)]
        NX = len(x_in)
        xth_flat = xt_hi[:, :, :].rearrange("p c t -> p (c t)")
        xtl_flat = xt_lo[:, :, :].rearrange("p c t -> p (c t)")
        WO = DCH * D_MODEL
        wo_hi = xth_flat[:, 0:WO].rearrange("p (c n) -> p c n", c=DCH)
        wo_lo = xtl_flat[:, 0:WO].rearrange("p (c n) -> p c n", c=DCH)
        MX = DCH * QT
        mx_hi = [xth_flat[:, WO + i * MX:WO + (i + 1) * MX].rearrange("p (c t) -> p c t", c=DCH) for i in range(2)]
        mx_lo = [xtl_flat[:, WO + i * MX:WO + (i + 1) * MX].rearrange("p (c t) -> p c t", c=DCH) for i in range(2)]
        rows = [buf[:, h * D_MODEL:(h + 1) * D_MODEL] for buf in (b_gate, z_conv) for h in range(2)]
        gain = z_attn[:, 0:D_MODEL]
        bias = z_attn[:, D_MODEL:2 * D_MODEL]
        NR = len(rows)

        consts_done = sem("consts_done")
        rows_done = sem("rows_done")
        taps_loaded = sem("taps_loaded")
        x_loaded = [sem(f"x_loaded{i}") for i in range(NX)]
        xh_done, xl_done = sem("xh_done"), sem("xl_done")
        w_loaded = [sem(f"w_loaded{i}") for i in range(2)]
        w_part = sem("w_part")
        w_ready = sem("w_ready")
        unit_done = sem("unit_done")
        proj_free = [sem(f"proj_free{i}") for i in range(2)]
        hi_done = sem("hi_done")
        z_ready = sem("z_ready")
        min_done, exp1_done, ln_done = sem("min_done"), sem("exp1_done"), sem("ln_done")
        sp_done, sph_done, spl_done = sem("sp_done"), sem("sph_done"), sem("spl_done")
        sums_ready, chi_done, carry_done = sem("sums_ready"), sem("chi_done"), sem("carry_done")
        arg_ready = sem("arg_ready")
        wt_done, wth_done, wtl_done = sem("wt_done"), sem("wth_done"), sem("wtl_done")
        pv_done = sem("pv_done")
        o_taken, omh_done, oml_done = sem("o_taken"), sem("omh_done"), sem("oml_done")
        om_stored = sem("om_stored")
        gate_in = sem("gate_in")
        u_done = sem("u_done")
        silu_done = sem("silu_done")
        y_step, gates_done, mixed, cmh_done, cml_done = (sem(n) for n in
                                                         ("y_step", "gates_done", "mixed", "cmh_done", "cml_done"))
        cm_stored = sem("cm_stored")
        wo_loaded = [sem(f"wo_loaded{i}") for i in range(2)]
        woh_done, wol_done = sem("woh_done"), sem("wol_done")
        affine_loaded = sem("affine_loaded")
        mx_loaded = [sem(f"mx_loaded{i}") for i in range(2)]
        row_loaded = [sem(f"row_loaded{i}") for i in range(NR)]
        row_scaled, sub_ready, row_summed = sem("row_scaled"), sem("sub_ready"), sem("row_summed")
        stats_done, var_done, log_done, rstd_done = (sem(n) for n in
                                                     ("stats_done", "var_done", "log_done", "rstd_done"))
        norm_step, row_done = sem("norm_step"), sem("row_done")
        row_stored = [sem(f"row_stored{i}") for i in range(NR)]

        block = ctx.enter_context(nc.Block())

        ARG_CREDIT, PV_CREDIT, WTL_CREDIT, O_CREDIT, CML_CREDIT = 2, 2, 1, 1, 1
        STORE_CREDIT = 32
        N_CONSTS, N_ROWS = 8 + 3, 9

        units_mid, steps_mid = schedule(False)
        units_last, steps_last = schedule(True)

        def plan(last):
            return (units_last, steps_last) if last else (units_mid, steps_mid)

        def unit_ends(last):
            _, steps = plan(last)
            ends = [[] for _ in range(NB + 1)]
            for n, mine in enumerate(steps):
                ends[n] += [u for u, i in mine if i == PIECES - 1]
            return ends

        def end_of(last, unit):
            return next(n for n, us in enumerate(unit_ends(last)) if unit in us)

        def split_steps(last):
            out = [[] for _ in range(NB + 1)]
            freed_by = {1: 0, 2: 1, 3: 2, 4: 6, 5: 10, 6: 14, 7: 18, 8: 22}
            for j, unit in freed_by.items():
                if not last or j <= 4:
                    out[end_of(last, unit)].append(j)
            return out

        def conv_events(n, last):
            first = end_of(last, LAST_UNIT_ZC) + 1
            gap = 1 if last else 2
            out = []
            for t in range(NQT):
                if min(first + gap * t, NB) == n:
                    out.append(("start", t))
                if min(first + gap * t + 1, NB) == n:
                    out.append(("finish", t))
            return sorted(out, key=lambda e: (e[1], e[0] == "finish"))

        GROUPS = [G_ZA, G_C, G_H, G_B, G_ZC, G_Q, G_K, G_V, G_ZA, G_C]

        def load_group(sp_eng, g_index, slot, group, pair):
            sp_eng.dma_start(w_raw[:, slot, :, :].rearrange("p c m -> p (c m)"), w_blocks[group, pair])\
                .then_inc(w_loaded[slot], 16)

        @block.sync
        def _(eng):
            for i, g in enumerate((G_Q, G_K)):
                load_group(eng, i, i, g, 0)
            for k in range(NX):
                eng.dma_start(x_in[k], x_blocks[NTB - 1 - k]).then_inc(x_loaded[k], 16)
            eng.wait_ge(w_ready, 1)
            load_group(eng, 2, 0, G_V, 0)
            eng.dma_start(taps[:, :, :], conv_taps_in).then_inc(taps_loaded, 16)
            for k in range(NX, NTB):
                if k == NX + 2:
                    eng.wait_ge(w_ready, 2)
                    load_group(eng, 3, 1, G_ZA, 0)
                eng.wait_ge(xh_done, k - NX + 1)
                eng.wait_ge(xl_done, k - NX + 1)
                eng.dma_start(x_in[k % NX], x_blocks[NTB - 1 - k]).then_inc(x_loaded[k % NX], 16)
            eng.wait_ge(w_ready, 3)
            load_group(eng, 4, 0, G_C, 0)

            def pair_stores(p, last):
                splits = split_steps(last)
                for n in range(NB + 1):
                    for j in splits[n]:
                        if j + 1 <= (4 if last else 9) and j + 1 >= 2:
                            g = 3 + (j + 1)
                            eng.wait_ge(w_ready, p * 8 + (g - 2 + 1))
                            load_group(eng, g, g % 2, GROUPS[j + 1], p + (1 if j + 1 >= 5 else 0))
                    for what, t in conv_events(n, last):
                        if what == "start":
                            continue
                        eng.wait_ge(cml_done, p * NQT + (t + 1 + CML_CREDIT))
                        eng.dma_start(mix_hi[p, :, t * QT:(t + 1) * QT], cm_hi[:, :]).then_inc(cm_stored, 16)
                        eng.dma_start(mix_lo[p, :, t * QT:(t + 1) * QT], cm_lo[:, :]).then_inc(cm_stored, 16)
                    if n - 1 in TILE_END:
                        t = TILE_END[n - 1]
                        k = NQT - 1 - t
                        eng.wait_ge(oml_done, p * NQT + (k + 1))
                        eng.dma_start(mix_hi[p + PAIRS, :, t * QT:(t + 1) * QT], om_hi[:, :]).then_inc(om_stored, 16)
                        eng.dma_start(mix_lo[p + PAIRS, :, t * QT:(t + 1) * QT], om_lo[:, :]).then_inc(om_stored, 16)

            for p in range(PAIRS):
                pair_stores(p, p == PAIRS - 1)

            for c in range(DCH):
                if c < 2:
                    eng.wait_ge(w_ready, 3 + 8 * (PAIRS - 1) + 5)
                else:
                    eng.wait_ge(wol_done, c - 1)
                eng.dma_start(w_raw[:, c % 2, :, :].rearrange("p c m -> p (c m)"), wo_rows[c])\
                   .then_inc(wo_loaded[c % 2], 16)
            eng.wait_ge(om_stored, STORE_CREDIT + 32 * NQT * PAIRS)
            eng.wait_ge(cm_stored, STORE_CREDIT + 32 * NQT * PAIRS)
            for name, dst in ((ln_gain, gain), (ln_bias, bias)):
                eng.dma_start(dst, name[0:1, :].broadcast_to([PART, D_MODEL])).then_inc(affine_loaded, 16)

            def load_mixed(s, i):
                for src, dst in ((mix_hi, mx_hi[i]), (mix_lo, mx_lo[i])):
                    eng.dma_start(dst, src.rearrange("c p t -> p c t")[:, :, bass.ds(s * QT, QT)])\
                       .then_inc(mx_loaded[i], 16)

            def load_row(r, i):
                eng.dma_start(rows[i], x_rows[r]).then_inc(row_loaded[i], 16)

            for i in range(2):
                load_mixed(i, i)
            for i in range(NR):
                load_row(i, i)
            for r in range(NTB):
                i = r % NR
                eng.wait_ge(row_done, r + 1)
                eng.dma_start(out_rows[r], rows[i]).then_inc(row_stored[i], 16)
                if r % SUB == SUB - 1 and r // SUB + 2 < NQT:
                    load_mixed(r // SUB + 2, r // SUB % 2)
                if r >= 1 and r - 1 + NR < NTB:
                    eng.wait_ge(row_stored[(r - 1) % NR], 16 * ((r - 1) // NR + 1))
                    load_row(r - 1 + NR, (r - 1) % NR)
            for i in range(NR):
                eng.wait_ge(row_stored[i], 16 * (NTB // NR))

        @block.tensor
        def _(pe):
            mm = nc.tensor.matmul

            def unit_products(unit):
                group, t, slot = unit
                prods = []
                if group == G_V:
                    for s in range(SUB):
                        tok = slice(t * QT + s * PART, t * QT + (s + 1) * PART)
                        for d in range(DCH):
                            for a, b in ((xt_hi, w_hi), (xt_hi, w_lo), (xt_lo, w_hi)):
                                prods.append((slice(s * PART, (s + 1) * PART), a[:, d, tok], b[:, slot, d, :],
                                              d == 0 and a is xt_hi and b is w_hi,
                                              d == DCH - 1 and a is xt_lo))
                else:
                    tok = slice(t * QT, (t + 1) * QT)
                    for d in range(DCH):
                        for a, b in ((w_hi, xt_hi), (w_hi, xt_lo), (w_lo, xt_hi)):
                            prods.append((slice(0, QT), a[:, slot, d, :], b[:, d, tok],
                                          d == 0 and a is w_hi and b is xt_hi,
                                          d == DCH - 1 and a is w_lo))
                return prods

            def unit_piece(p, index, unit, piece, wait_weights):
                prods = unit_products(unit)
                size = len(prods) // PIECES
                bank = (N_FIRST + index) % 2
                if piece == 0:
                    if wait_weights is not None:
                        pe.wait_ge(w_ready, wait_weights)
                    uses = (N_FIRST + index) // 2
                    if index >= 0 or uses > 0:
                        pe.wait_ge(proj_free[bank], p * (N_UNITS // 2) + uses)
                for cols, lhs, rhs, start, stop in prods[piece * size:(piece + 1) * size]:
                    last = mm(proj[bank][:, cols], lhs, rhs, start=start, stop=stop)
                if piece == PIECES - 1:
                    last.then_inc(unit_done, 1)

            pe.wait_ge(consts_done, N_CONSTS)
            pe.wait_ge(rows_done, N_ROWS)
            for tile in range(NQT):
                if tile < NQT - 1:
                    pe.wait_ge(xl_done, (tile + 1) * SUB)
                    pe.wait_ge(xh_done, (tile + 1) * SUB)
                    for g in range(3):
                        i = 3 * tile + g
                        for piece in range(PIECES):
                            unit_piece(0, i - N_FIRST, UNITS_FIRST[i], piece, g + 1 if tile == 0 else None)
            pe.wait_ge(xl_done, NTB)
            pe.wait_ge(xh_done, NTB)

            first_of_group = {3: 0, 7: 1, 11: 2, 15: 3, 19: 4, 23: 5, 24: 6, 25: 7}

            def pair_products(p, last):
                units, steps = plan(last)

                def pieces(todo):
                    for u, i in todo:
                        j = first_of_group.get(u)
                        weights = None if j is None else p * 8 + (3 + j + 1)
                        unit_piece(p, u, units[u], i, weights)

                def taken(p, units_before):
                    for bank in range(2):
                        pe.wait_ge(proj_free[bank], p * (N_UNITS // 2) + (units_before + 1 - bank) // 2)

                def scores(n):
                    t, b, c0 = BLOCKS[n]
                    pe.wait_ge(wt_done, p * NB + (n - 2 + 1 + ARG_CREDIT))
                    if n == 0:
                        taken(p, N_FIRST)
                    if (t, b) == (NQT - 1, SUB - 1):
                        taken(p, N_FIRST + 3)
                    keys = slice(b * PART, (b + 1) * PART)
                    cols = slice(t * QT + c0, (t + 1) * QT)
                    diagonal = b >= SUB * t
                    for i, (a, c) in enumerate(((k_hi, q_hi), (k_hi, q_lo), (k_lo, q_hi))):
                        for h in range(2):
                            rows_h = slice(h * HEAD_DIM, (h + 1) * HEAD_DIM)
                            last_mm = mm(arg[n % 2][:, h, c0:QT], a[rows_h, keys], c[rows_h, cols],
                                         start=(i == 0), stop=(i == 2), skip_group_check=True)
                    if diagonal:
                        for h in range(2):
                            last_mm = mm(arg[n % 2][:, h, c0:c0 + PART], root_id[:, :], future[:, :],
                                         start=False, stop=True, skip_group_check=True)
                    last_mm.then_inc(z_ready, 1)

                def carried(n):
                    t, b, c0 = BLOCKS[n]
                    if b == SUB * (t + 1) - 1:
                        return
                    pe.wait_ge(carry_done, p * SUMS + SUMS_BEFORE[n])
                    c1 = BLOCKS[n - 1][2]
                    for h in range(2):
                        rows_h = slice(h * HEAD_DIM, (h + 1) * HEAD_DIM)
                        mm(arg[n % 2][:, h, c1:QT], spread[rows_h, :], carry[rows_h, c1:QT],
                           start=False, stop=True, skip_group_check=True)

                def sums_within(n):
                    t, b, c0 = BLOCKS[n]
                    pe.wait_ge(spl_done, p * NB + (n + 1))
                    carried(n)
                    first = b == SUB * (t + 1) - 1
                    if b > 0:
                        for part in (sp_hi, sp_lo):
                            for h in range(2):
                                last_mm = mm(sums[h * HEAD_DIM:(h + 1) * HEAD_DIM, c0:QT], ones[:, :],
                                             part[:, h, c0:QT], start=(first and part is sp_hi), stop=True,
                                             skip_group_check=True)
                        last_mm.then_inc(sums_ready, 1)
                    for part in (sp_hi, sp_lo):
                        for h in range(2):
                            last_mm = mm(arg[n % 2][:, h, c0:QT], tri[:, :], part[:, h, c0:QT],
                                         start=False, stop=True, skip_group_check=True)
                    last_mm.then_inc(arg_ready, 1)

                def values(n):
                    t, b, c0 = BLOCKS[n]
                    pe.wait_ge(wtl_done, p * NB + (n + 1 + WTL_CREDIT))
                    first = b == SUB * (t + 1) - 1
                    if first:
                        pe.wait_ge(o_taken, p * NQT + (NQT - 1 - t + O_CREDIT))
                    for i, (a, c) in enumerate(((v_hi, wt_hi), (v_hi, wt_lo), (v_lo, wt_hi))):
                        for h in range(2):
                            cols_h = slice(h * HEAD_DIM, (h + 1) * HEAD_DIM)
                            last_mm = mm(o_acc[cols_h, c0:QT], a[:, b, cols_h], c[:, n % 2, h, c0:QT],
                                         start=(first and i == 0), stop=(i == 2), skip_group_check=True)
                    last_mm.then_inc(pv_done, 1)

                scores(0)
                for n in range(NB):
                    half = (len(steps[n]) + 1) // 2
                    if n + 1 < NB:
                        scores(n + 1)
                    pieces(steps[n][:half])
                    sums_within(n)
                    pieces(steps[n][half:])
                    if n >= 1:
                        values(n - 1)
                pieces(steps[NB])
                values(NB - 1)

            with pe.Fori(0, PAIRS - 1) as p:
                pair_products(p, False)
            pair_products(PAIRS - 1, True)

            pe.wait_ge(wol_done, DCH)
            with pe.Fori(0, NQT // 2) as s2:
                for k in range(2 * SUB):
                    i, s = k // SUB, k % SUB
                    if s == 0:
                        pe.wait_ge(mx_loaded[i], s2 * 32 + 32)
                    pe.wait_ge(row_summed, s2 * (2 * SUB) + (k - 2 + 1 + 2))
                    for half in range(2):
                        for c in range(DCH):
                            for m, (a, b) in enumerate(((mx_hi[i], wo_hi), (mx_hi[i], wo_lo), (mx_lo[i], wo_hi))):
                                last = mm(arg[k % 2][:, half, :], a[:, c, s * PART:(s + 1) * PART],
                                          b[:, c, half * QT:(half + 1) * QT],
                                          start=(c == 0 and m == 0), stop=(c == DCH - 1 and m == 2))
                    last.then_inc(sub_ready, 1)

        def high_place(unit):
            group, t, _ = unit
            tok = slice(t * QT, (t + 1) * QT)
            if group == G_V:
                return (v_hi[:, t * SUB:(t + 1) * SUB, :].rearrange("p s c -> p (s c)"),
                        v_lo[:, t * SUB:(t + 1) * SUB, :].rearrange("p s c -> p (s c)"))
            return (q_hi[:, tok], q_lo[:, tok]) if group == G_Q else (k_hi[:, tok], k_lo[:, tok])

        def first_hi(act, i):
            act.wait_ge(unit_done, i + 1)
            nc.scalar.activation(high_place(UNITS_FIRST[i])[0], proj[i % 2][:, :], ACT.Copy, scale=PROJ_SCALE)\
                .then_inc(hi_done, 1)

        def hi_count(u):
            return u + 1 if u < 3 else 3 + (u - len(UNITS_IN)) + 1

        def take_unit(act, p, u, unit):
            group, t, _ = unit
            bank = (N_FIRST + u) % 2
            tok = slice(t * QT, (t + 1) * QT)
            if group == G_H:
                return
            act.wait_ge(unit_done, p * N_UNITS + (N_FIRST + u + 1))
            if group in (G_Q, G_K, G_V):
                nc.scalar.activation(high_place(unit)[0], proj[bank][:, :], ACT.Copy, scale=PROJ_SCALE)\
                    .then_inc(hi_done, 1)
                return
            dst = {G_ZA: z_attn[:, tok], G_B: b_gate[:, tok], G_ZC: z_conv[:, tok],
                   G_C: u_conv[:, CONV_K - 1 + t * QT:CONV_K - 1 + (t + 1) * QT]}[group]
            nc.scalar.activation(dst, proj[bank][:, :], ACT.Copy, scale=PROJ_SCALE).then_inc(proj_free[bank], 1)
            if t == NQT - 1 and group in (G_ZA, G_ZC):
                gate = z_attn if group == G_ZA else z_conv
                for bk, back in ((bank, 0), (1 - bank, 1)):
                    act.wait_ge(proj_free[bk], p * (N_UNITS // 2) + ((N_FIRST + u - back) // 2 + 1))
                nc.scalar.activation(gate[:, :], gate[:, :], ACT.Silu).then_inc(silu_done, 1)
                nc.scalar.preload_act_table_set(TABLES)

        @block.scalar
        def _(act):
            act.wait_ge(consts_done, N_CONSTS)
            nc.scalar.preload_act_table_set(TABLES)
            for k in range(NTB):
                act.wait_ge(x_loaded[k % NX], 16 * (k // NX + 1))
                blk = NTB - 1 - k
                nc.scalar.activation(xt_hi[:, :, blk * PART:(blk + 1) * PART],
                                     x_in[k % NX].rearrange("p (c t) -> p c t", t=PART),
                                     ACT.Copy, scale=X_SCALE).then_inc(xh_done, 1)
                if k % SUB == SUB - 1 and k < NTB - 1:
                    for g in range(3):
                        first_hi(act, 3 * (k // SUB) + g)

            def pair_activations(p, last):
                units, _ = plan(last)
                ends = unit_ends(last)

                def softplus_terms(n):
                    c0 = BLOCKS[n][2]
                    e = sp[:, n % 2, :, c0:QT]
                    act.wait_ge(min_done, p * NB + (n + 1))
                    nc.scalar.activation(e, e, ACT.Exp).then_inc(exp1_done, 1)
                    act.wait_ge(exp1_done, p * NB + (n + 1))
                    nc.scalar.activation(e, e, ACT.Ln, bias=1.0).then_inc(ln_done, 1)

                softplus_terms(0)
                for n in range(NB + 1):
                    if n < NB:
                        c0 = BLOCKS[n][2]
                        act.wait_ge(sp_done, p * NB + (n + 1))
                        nc.scalar.activation(sp_hi[:, :, c0:QT], sp[:, n % 2, :, c0:QT], ACT.Copy)\
                            .then_inc(sph_done, 1)
                        if n + 1 < NB:
                            softplus_terms(n + 1)
                        act.wait_ge(arg_ready, p * NB + (n + 1))
                        act.wait_ge(wtl_done, p * NB + (n + WTL_CREDIT))
                        nc.scalar.activation(wt[:, :, c0:QT], arg[n % 2][:, :, c0:QT], ACT.Exp,
                                             bias=p_bias[:, :], scale=1.0 / ROOT).then_inc(wt_done, 1)
                        act.wait_ge(wt_done, p * NB + (n + 1 + ARG_CREDIT))
                        act.wait_ge(pv_done, p * NB + (n - 2 + 1 + PV_CREDIT))
                        nc.scalar.activation(wt_hi[:, n % 2, :, c0:QT], wt[:, :, c0:QT], ACT.Copy)\
                            .then_inc(wth_done, 1)
                    for u in ends[n]:
                        take_unit(act, p, u, units[u])

            with act.Fori(0, PAIRS - 1) as p:
                pair_activations(p, False)
            pair_activations(PAIRS - 1, True)

            for c in range(DCH):
                act.wait_ge(wo_loaded[c % 2], 16 * (c // 2 + 1))
                if c == 0:
                    act.wait_ge(unit_done, N_FIRST + N_UNITS * (PAIRS - 1) + len(units_last))
                nc.scalar.activation(wo_hi[:, c, :], w_raw[:, c % 2, :, :].rearrange("p c m -> p (c m)"),
                                     ACT.Copy, scale=W_SCALE).then_inc(woh_done, 1)
            with act.Fori(0, NQT // 2) as s2:
                for k in range(2 * SUB):
                    i = k % NR
                    act.wait_ge(row_loaded[i], s2 * (16 * 2 * SUB // NR) + 16 * (k // NR + 1))
                    nc.scalar.activation(rows[i], rows[i], ACT.Copy, scale=ALPHA).then_inc(row_scaled, 1)
                    act.wait_ge(var_done, s2 * (2 * SUB) + (k + 1))
                    nc.scalar.activation(log_var[:, k % 2:k % 2 + 1], mean_var[:, k % 2, 1:2], ACT.Ln,
                                         bias=eps[:, :]).then_inc(log_done, 1)
                    act.wait_ge(log_done, s2 * (2 * SUB) + (k + 1))
                    nc.scalar.activation(rstd[:, k % 2:k % 2 + 1], log_var[:, k % 2:k % 2 + 1], ACT.Exp,
                                         scale=-0.5).then_inc(rstd_done, 1)

        def first_low(dve, i):
            dve.wait_ge(hi_done, i + 1)
            hi, lo = high_place(UNITS_FIRST[i])
            nc.vector.scalar_tensor_tensor(out=lo, in0=proj[i % 2][:, :], scalar=PROJ_SCALE, in1=hi, op0=ALU.mult,
                                           op1=ALU.subtract).then_inc(proj_free[i % 2], 1)

        @block.vector
        def _(dve):
            stt = nc.vector.scalar_tensor_tensor

            nc.vector.memset(spread[:, :], 0.0).then_inc(rows_done, 1)
            dve.wait_ge(rows_done, 1)
            for i in range(4):
                nc.vector.memset(spread[32 * i:32 * i + 1, :], -ROOT).then_inc(rows_done, 1)
                nc.vector.memset(low_rows[32 * i:32 * i + 32, :], float(i % 2)).then_inc(rows_done, 1)
            dve.wait_ge(consts_done, N_CONSTS)
            dve.wait_ge(rows_done, N_ROWS)
            dve.wait_ge(taps_loaded, 16)
            for k in range(NTB):
                dve.wait_ge(xh_done, k + 1)
                blk = NTB - 1 - k
                cols = slice(blk * PART, (blk + 1) * PART)
                stt(out=xt_lo[:, :, cols], in0=x_in[k % NX].rearrange("p (c t) -> p c t", t=PART),
                    scalar=X_SCALE, in1=xt_hi[:, :, cols], op0=ALU.mult, op1=ALU.subtract).then_inc(xl_done, 1)
                if k % SUB == SUB - 1 and k < NTB - 1:
                    for g in range(3):
                        first_low(dve, 3 * (k // SUB) + g)

            def pair_vectors(p, last):
                units, _ = plan(last)
                ends = unit_ends(last)

                def clamp(n):
                    c0 = BLOCKS[n][2]
                    dve.wait_ge(z_ready, p * NB + (n + 1))
                    nc.vector.tensor_scalar(sp[:, n % 2, :, c0:QT], arg[n % 2][:, :, c0:QT], 1.0 / ROOT, EXP_CLAMP,
                                            ALU.mult, ALU.min).then_inc(min_done, 1)

                def softplus_guard(n):
                    c0 = BLOCKS[n][2]
                    dve.wait_ge(ln_done, p * NB + (n + 1))
                    stt(out=sp[:, n % 2, :, c0:QT], in0=arg[n % 2][:, :, c0:QT], scalar=1.0 / ROOT,
                        in1=sp[:, n % 2, :, c0:QT], op0=ALU.mult, op1=ALU.max).then_inc(sp_done, 1)

                def softplus_low(n):
                    c0 = BLOCKS[n][2]
                    dve.wait_ge(sph_done, p * NB + (n + 1))
                    nc.vector.tensor_tensor(sp_lo[:, :, c0:QT], sp[:, n % 2, :, c0:QT], sp_hi[:, :, c0:QT],
                                            ALU.subtract).then_inc(spl_done, 1)

                def split_carry(n):
                    _, b, c0 = BLOCKS[n]
                    if b == 0:
                        return
                    dve.wait_ge(sums_ready, p * SUMS + (SUMS_BEFORE[n] + 1))
                    nc.vector.tensor_scalar(carry_hi[:, c0:QT], sums[:, c0:QT], CUT, low_rows[:, :],
                                            ALU.min, ALU.mult).then_inc(chi_done, 1)
                    dve.wait_ge(chi_done, p * SUMS + (SUMS_BEFORE[n] + 1))
                    stt(out=carry[:, c0:QT], in0=sums[:, c0:QT], scalar=CUT, in1=carry_hi[:, c0:QT],
                        op0=ALU.min, op1=ALU.subtract).then_inc(carry_done, 1)

                def take(u):
                    group, t, _ = units[u]
                    bank = (N_FIRST + u) % 2
                    if group == G_H:
                        dve.wait_ge(unit_done, p * N_UNITS + (N_FIRST + u + 1))
                        if t == 0:
                            for bk in range(2):
                                last_c = max(v for v in range(u) if (N_FIRST + v) % 2 == bk)
                                dve.wait_ge(proj_free[bk], p * (N_UNITS // 2) + ((N_FIRST + last_c) // 2 + 1))
                        at = u_conv[:, CONV_K - 1 + t * QT:CONV_K - 1 + (t + 1) * QT]
                        stt(out=at, in0=proj[bank][:, :], scalar=PROJ_SCALE, in1=at, op0=ALU.mult, op1=ALU.mult)\
                            .then_inc(proj_free[bank], 1)
                    elif group in (G_Q, G_K, G_V):
                        dve.wait_ge(hi_done, p * 12 + (9 + hi_count(u)))
                        hi, lo = high_place(units[u])
                        stt(out=lo, in0=proj[bank][:, :], scalar=PROJ_SCALE, in1=hi, op0=ALU.mult,
                            op1=ALU.subtract).then_inc(proj_free[bank], 1)

                def conv_taps(t):
                    if t == 0:
                        for bk in range(2):
                            last_h = max(v for v in range(15) if (N_FIRST + v) % 2 == bk)
                            dve.wait_ge(proj_free[bk], p * (N_UNITS // 2) + ((N_FIRST + last_h) // 2 + 1))
                    dve.wait_ge(cml_done, p * NQT + (t + CML_CREDIT))
                    base = t * QT
                    nc.vector.tensor_scalar(y_conv[:, :], u_conv[:, base + 2:base + 2 + QT], taps[:, bass.ds(p, 1), 2],
                                            None, ALU.mult).then_inc(y_step, 1)
                    for j in (1, 0):
                        dve.wait_ge(y_step, p * (3 * NQT) + (3 * t + 2 - j))
                        stt(out=y_conv[:, :], in0=u_conv[:, base + j:base + j + QT], scalar=taps[:, bass.ds(p, 1), j],
                            in1=y_conv[:, :], op0=ALU.mult, op1=ALU.add).then_inc(y_step, 1)

                def conv_high(t):
                    dve.wait_ge(mixed, p * NQT + (t + 1))
                    dve.wait_ge(cm_stored, p * (32 * NQT) + (32 * t + STORE_CREDIT))
                    nc.vector.tensor_copy(cm_hi[:, :], y_conv[:, :]).then_inc(cmh_done, 1)

                def take_output(t):
                    k = NQT - 1 - t
                    n = next(m for m, tt in TILE_END.items() if tt == t)
                    dve.wait_ge(pv_done, p * NB + (n + 1 + PV_CREDIT))
                    if k == 0:
                        dve.wait_ge(silu_done, p * 2 + 1)
                    dve.wait_ge(om_stored, p * (32 * NQT) + (32 * k + STORE_CREDIT))
                    stt(out=o_gated[:, :], in0=o_acc[:, :], scalar=1.0 / P_SCALE,
                        in1=z_attn[:, t * QT:(t + 1) * QT], op0=ALU.mult, op1=ALU.mult).then_inc(o_taken, 1)
                    dve.wait_ge(o_taken, p * NQT + (k + 1 + O_CREDIT))
                    nc.vector.tensor_copy(om_hi[:, :], o_gated[:, :]).then_inc(omh_done, 1)

                clamp(0)
                for n in range(NB + 1):
                    if n < NB:
                        softplus_guard(n)
                        if n + 1 < NB:
                            clamp(n + 1)
                        softplus_low(n)
                        split_carry(n)
                    for u in ends[n]:
                        take(u)
                    for what, t in conv_events(n, last):
                        (conv_taps if what == "start" else conv_high)(t)
                    if n - 1 in TILE_END:
                        take_output(TILE_END[n - 1])

            with dve.Fori(0, PAIRS - 1) as p:
                pair_vectors(p, False)
            pair_vectors(PAIRS - 1, True)

            for c in range(DCH):
                dve.wait_ge(woh_done, c + 1)
                stt(out=wo_lo[:, c, :], in0=w_raw[:, c % 2, :, :].rearrange("p c m -> p (c m)"), scalar=W_SCALE,
                    in1=wo_hi[:, c, :], op0=ALU.mult, op1=ALU.subtract).then_inc(wol_done, 1)
            dve.wait_ge(affine_loaded, 32)
            with dve.Fori(0, NQT // 2) as s2:
                for k in range(2 * SUB):
                    i = k % NR
                    this = s2 * (2 * SUB) + (k + 1)
                    dve.wait_ge(sub_ready, this)
                    dve.wait_ge(row_scaled, this)
                    stt(out=rows[i], in0=arg[k % 2][:, :, :].rearrange("p h n -> p (h n)"),
                        scalar=1.0 / W_SCALE, in1=rows[i], op0=ALU.mult, op1=ALU.add).then_inc(row_summed, 1)
                    dve.wait_ge(row_summed, s2 * (2 * SUB) + (k + 1 + 2))
                    for half in range(2):
                        nc.vector.bn_stats(stats[:, k % 2, 6 * half:6 * half + 6], rows[i][:, half * QT:(half + 1) * QT])\
                            .then_inc(stats_done, 1)
                    dve.wait_ge(stats_done, s2 * (4 * SUB) + 2 * (k + 1))
                    nc.vector.memset(given[:, 0:1], 0.0)
                    nc.vector.bn_aggr(mean_var[:, k % 2, :], stats[:, k % 2, :]).then_inc(var_done, 1)
                    dve.wait_ge(var_done, this)
                    dve.wait_ge(rstd_done, this)
                    nc.vector.tensor_scalar(rows[i], rows[i], mean_var[:, k % 2, 0:1], rstd[:, k % 2:k % 2 + 1],
                                            ALU.subtract, ALU.mult).then_inc(norm_step, 1)
                    dve.wait_ge(norm_step, s2 * (4 * SUB) + (2 * k + 1))
                    nc.vector.tensor_tensor(rows[i], rows[i], gain, ALU.mult).then_inc(norm_step, 1)
                    dve.wait_ge(norm_step, s2 * (4 * SUB) + (2 * k + 2))
                    nc.vector.tensor_tensor(rows[i], rows[i], bias, ALU.add).then_inc(row_done, 1)

        @block.gpsimd
        def _(pool):
            below = dict(pattern=[[-1, PART]], base=0, channel_multiplier=1)
            credits = [(wt_done, ARG_CREDIT), (pv_done, PV_CREDIT), (wtl_done, WTL_CREDIT), (o_taken, O_CREDIT),
                       (cml_done, CML_CREDIT), (om_stored, STORE_CREDIT), (cm_stored, STORE_CREDIT), (row_summed, 2)]
            for i, (what, n) in enumerate(credits):
                nc.gpsimd.memset(given[:, i:i + 1], 0.0).then_inc(what, n)
            fills = [(tri[:, :], -ROOT), (future[:, :], -CUT), (root_id[:, :], 0.0),
                     (ones[:, :], 1.0), (p_bias[:, :], math.log(P_SCALE)),
                     (eps[:, :], LN_EPS), (w_scale[:, :], W_SCALE), (u_conv[:, 0:CONV_K - 1], 0.0)]
            for dst, value in fills:
                nc.gpsimd.memset(dst, value).then_inc(consts_done, 1)
            pool.wait_ge(consts_done, len(fills))
            for dst in (tri, future):
                nc.gpsimd.affine_select(out=dst[:, :], in_=dst[:, :], compare_op=ALU.is_ge, fill=0.0, **below)\
                    .then_inc(consts_done, 1)
            for dst, value in ((root_id, ROOT),):
                nc.gpsimd.affine_select(out=dst[:, :], in_=dst[:, :], compare_op=ALU.not_equal, fill=value, **below)\
                    .then_inc(consts_done, 1)

            def split_weights(slot, raw, loaded, ready_before):
                pool.wait_ge(w_loaded[raw], loaded)
                flat = lambda a: a.rearrange("p c m -> p (c m)")
                w = flat(w_raw[:, raw, :, :])
                hi, lo = flat(w_hi[:, slot, :, :]), flat(w_lo[:, slot, :, :])
                nc.gpsimd.tensor_tensor(hi, w, w_scale[:, 0:1].broadcast_to([PART, D_MODEL]), ALU.mult)\
                    .then_inc(w_part, 1)
                nc.gpsimd.tensor_scalar(w, w, W_SCALE, 1.0, ALU.mult, ALU.mult).then_inc(w_part, 1)
                pool.wait_ge(w_part, ready_before)
                nc.gpsimd.tensor_tensor(lo, w, hi, ALU.subtract).then_inc(w_ready, 1)

            for g in range(4):
                split_weights(g, g % 2, 16 * (g // 2 + 1), 2 * (g + 1))

            def pair_pool(p, last):
                splits = split_steps(last)
                for n in range(NB + 1):
                    if n < NB:
                        c0 = BLOCKS[n][2]
                        pool.wait_ge(wth_done, p * NB + (n + 1))
                        nc.gpsimd.tensor_tensor(wt_lo[:, n % 2, :, c0:QT], wt[:, :, c0:QT],
                                                wt_hi[:, n % 2, :, c0:QT], ALU.subtract).then_inc(wtl_done, 1)
                    for j in splits[n]:
                        g = 3 + j
                        unit = {1: 0, 2: 1, 3: 2, 4: 6, 5: 10, 6: 14, 7: 18, 8: 22}[j]
                        pool.wait_ge(unit_done, p * N_UNITS + (N_FIRST + unit + 1))
                        split_weights(g % 4, g % 2, p * 64 + 16 * (g // 2 + 1), p * 16 + 2 * (g + 1))
                    for what, t in conv_events(n, last):
                        tok = slice(t * QT, (t + 1) * QT)
                        if what == "start":
                            if t == 0:
                                pool.wait_ge(silu_done, p * 2 + 2)
                            nc.gpsimd.tensor_tensor(b_gate[:, tok], b_gate[:, tok], z_conv[:, tok], ALU.mult)\
                                .then_inc(gates_done, 1)
                            pool.wait_ge(gates_done, p * NQT + (t + 1))
                            pool.wait_ge(y_step, p * (3 * NQT) + 3 * (t + 1))
                            nc.gpsimd.tensor_tensor(y_conv[:, :], y_conv[:, :], b_gate[:, tok], ALU.mult)\
                                .then_inc(mixed, 1)
                        else:
                            pool.wait_ge(cmh_done, p * NQT + (t + 1))
                            nc.gpsimd.tensor_tensor(cm_lo[:, :], y_conv[:, :], cm_hi[:, :], ALU.subtract)\
                                .then_inc(cml_done, 1)
                    if n - 1 in TILE_END:
                        k = NQT - 1 - TILE_END[n - 1]
                        pool.wait_ge(omh_done, p * NQT + (k + 1))
                        nc.gpsimd.tensor_tensor(om_lo[:, :], o_gated[:, :], om_hi[:, :], ALU.subtract)\
                            .then_inc(oml_done, 1)

            with pool.Fori(0, PAIRS - 1) as p:
                pair_pool(p, False)
            pair_pool(PAIRS - 1, True)


_OUT = ((1, SEQ, D_MODEL), "float32")


def kernel(**inputs):
    import numpy as _np
    import concourse.bacc as _bacc
    from concourse import mybir as _mybir
    from concourse.bass_utils import run_bass_kernel_spmd as _run

    nc = _bacc.Bacc("TRN2", target_bir_lowering=False, num_devices=1)
    arrays, args = {}, []
    laid_out = {
        "x": inputs["x"],
        "x_blocks": inputs["x"][0].reshape(NTB, PART, DCH, PART).transpose(0, 3, 2, 1).reshape(NTB, PART, D_MODEL),
        "w_blocks": inputs["w_in"][0].reshape(DCH, PART, 8, PAIRS, PART).transpose(2, 3, 1, 0, 4)
                    .reshape(8, PAIRS, PART, D_MODEL),
        "conv_taps": inputs["conv_w"][0].reshape(CONV_K, PAIRS, PART).transpose(2, 1, 0),
        "w_out": inputs["w_out"], "ln_gain": inputs["ln_gain"], "ln_bias": inputs["ln_bias"],
    }
    for name, laid in laid_out.items():
        a = _np.ascontiguousarray(laid)
        arrays[f"in_{name}_dram"] = a
        args.append(nc.dram_tensor(f"in_{name}_dram", a.shape, _mybir.dt.from_np(a.dtype), kind="ExternalInput").ap())
    shape, dtype = _OUT
    args.append(nc.dram_tensor("out_0_dram", shape, _mybir.dt.from_np(_np.dtype(dtype)), kind="ExternalOutput").ap())
    layer_program(nc, *args)
    r = _run(nc, [arrays], core_ids=[0])
    return r.results[0]["out_0_dram"]
```

```python
import math

import concourse.bass as bass
from concourse import mybir
from contextlib import ExitStack

F32 = mybir.dt.float32
F16 = mybir.dt.float16
ALU = mybir.AluOpType
ACT = mybir.ActivationFunctionType

SEQ, D_MODEL, PROJ = 2048, 1024, 4096
CONV_W = ATTN_W = 512
HEAD_DIM = 64
CONV_K = 3
LN_EPS = 1e-5
ALPHA = 2.0 ** 0.25
PART = 128
DCH = D_MODEL // PART
QT = 512
NQT = SEQ // QT
SUB = QT // PART
NTB = SEQ // PART
PAIRS = ATTN_W // PART
CUT = 60000.0
ROOT = 8.0
X_SCALE, W_SCALE, P_SCALE = 16.0, 512.0, 1024.0
PROJ_SCALE = 1.0 / (X_SCALE * W_SCALE)
EXP_CLAMP = 40.0
TABLES = "natural_log_exp_and_others"

G_B, G_C, G_H, G_ZC, G_Q, G_K, G_V, G_ZA = range(8)


def blocks_of_pair():
    out = []
    for t in reversed(range(NQT)):
        for b in reversed(range(SUB * (t + 1))):
            out.append((t, b, PART * max(0, b - SUB * t)))
    return out


BLOCKS = blocks_of_pair()
NB = len(BLOCKS)
SUMS_BEFORE = [sum(1 for _, b, _ in BLOCKS[:n] if b > 0) for n in range(NB + 1)]
SUMS = SUMS_BEFORE[NB]
TILE_END = {n: t for n, (t, b, _) in enumerate(BLOCKS) if b == 0}

UNITS_IN = [(G_Q, 0, 0), (G_K, 0, 1), (G_V, 0, 2)]
UNITS_IN += [(G_ZA, t, 3) for t in range(NQT)]
UNITS_IN += [(_g, t, _s) for t in reversed(range(NQT)) for _g, _s in ((G_C, 0), (G_H, 1), (G_B, 2), (G_ZC, 3))]
UNITS_NEXT = [(g, t, s) for t in (3, 2, 1) for g, s in ((G_Q, 0), (G_K, 1), (G_V, 2))]
UNITS_FIRST = UNITS_NEXT
N_FIRST, N_UNITS = len(UNITS_FIRST), len(UNITS_IN) + len(UNITS_NEXT)
G_OUT = 8
ROWS_EARLY = 2 * SUB
UNITS_OUT = [(G_OUT, r, h) for r in range(ROWS_EARLY) for h in range(2)]
PIECES = 6
STEP_COST, FIRST_COST, TAIL_COST = 350, 500, 250
LAST_UNIT_ZA, LAST_UNIT_ZC = 6, 22
FIRST_OF_GROUP = {3: 0, 7: 1, 8: 2, 9: 3, 10: 4, 23: 5, 24: 6, 25: 7}
FREED_BY = {1: 0, 2: 1, 3: 2, 4: 6, 5: 19, 6: 20, 7: 21, 8: 22}
LAST_UNIT_UPPER = 14
STEPS_IN_LAST = (0, 18)
STEPS_OUT_LAST = ((20, 29), (30, 40))


def step_of_end(tile):
    return max(m for m, t in TILE_END.items() if t == tile)


def spread_over(pieces, first, last, steps):
    cost = [QT - BLOCKS[n][2] + STEP_COST if n < NB else TAIL_COST for n in range(first, last + 1)]
    if first == 0:
        cost[0] += FIRST_COST
    done, at = 0, 0
    for n in range(first, last + 1):
        done += cost[n - first]
        want = round(len(pieces) * done / sum(cost))
        while at < want:
            u, _ = pieces[at]
            if len(UNITS_IN) <= u and last == NB and first == 0:
                if n < step_of_end(UNITS_NEXT[u - len(UNITS_IN)][1]) + 1:
                    break
            steps[n].append(pieces[at])
            at += 1
    assert at == len(pieces)


def schedule(last):
    units = UNITS_IN + (UNITS_OUT if last else UNITS_NEXT)
    pieces = [(u, i) for u in range(len(units)) for i in range(PIECES)]
    steps = [[] for _ in range(NB + 1)]
    if last:
        n_in, n_tile = len(UNITS_IN) * PIECES, 2 * SUB * PIECES
        spread_over(pieces[:n_in], *STEPS_IN_LAST, steps)
        spread_over(pieces[n_in:n_in + n_tile], *STEPS_OUT_LAST[0], steps)
        spread_over(pieces[n_in + n_tile:], *STEPS_OUT_LAST[1], steps)
    else:
        spread_over(pieces, 0, NB, steps)
    return units, steps


def layer_program(nc, x, x_blocks, w_blocks, conv_taps_in, w_out, ln_gain, ln_bias, out):
    mix_hi = nc.dram_tensor("mix_hi", [2 * PAIRS, PART, SEQ], F16, kind="Internal").ap()
    mix_lo = nc.dram_tensor("mix_lo", [2 * PAIRS, PART, SEQ], F16, kind="Internal").ap()
    x_rows = x[0].rearrange("(i p) d -> i p d", p=PART)
    out_rows = out[0].rearrange("(i p) d -> i p d", p=PART)
    wo_rows = w_out[0].rearrange("(c p) n -> c p n", p=PART)

    with ExitStack() as ctx:
        def sb(name, shape, dt):
            return ctx.enter_context(nc.sbuf_tensor(name, shape, dt))

        def sem(name):
            return ctx.enter_context(nc.semaphore(name))

        xt_hi = sb("xt_hi", [PART, DCH, SEQ], F16)
        xt_lo = sb("xt_lo", [PART, DCH, SEQ], F16)
        w_raw = sb("w_raw", [PART, 2, DCH, PART], F32)
        w_hi = sb("w_hi", [PART, 4, DCH, PART], F16)
        w_lo = sb("w_lo", [PART, 4, DCH, PART], F16)
        q_hi = sb("q_hi", [PART, SEQ], F16)
        q_lo = sb("q_lo", [PART, SEQ], F16)
        k_hi = sb("k_hi", [PART, SEQ], F16)
        k_lo = sb("k_lo", [PART, SEQ], F16)
        v_hi = sb("v_hi", [PART, NTB, PART], F16)
        v_lo = sb("v_lo", [PART, NTB, PART], F16)
        sp = sb("sp", [PART, 2, 2, QT], F32)
        sp_hi = sb("sp_hi", [PART, 2, 2, QT], F16)
        sp_lo = sb("sp_lo", [PART, 2, 2, QT], F16)
        wt = sb("wt", [PART, 2, QT], F32)
        wt_hi = sb("wt_hi", [PART, 2, 2, QT], F16)
        wt_lo = sb("wt_lo", [PART, 2, 2, QT], F16)
        carry_hi = sb("carry_hi", [PART, QT], F16)
        carry = sb("carry", [PART, QT], F16)
        u_conv = sb("u_conv", [PART, CONV_K - 1 + SEQ], F32)
        b_gate = sb("b_gate", [PART, SEQ], F32)
        z_conv = sb("z_conv", [PART, SEQ], F32)
        z_attn = sb("z_attn", [PART, SEQ], F32)
        y_conv = sb("y_conv", [PART, 2, QT], F32)
        cm_hi = sb("cm_hi", [PART, QT], F16)
        cm_lo = sb("cm_lo", [PART, QT], F16)
        o_gated = sb("o_gated", [PART, QT], F32)
        om_hi = sb("om_hi", [PART, QT], F16)
        om_lo = sb("om_lo", [PART, QT], F16)
        tri = sb("tri", [PART, PART], F16)
        future = sb("future", [PART, PART], F16)
        root_id = sb("root_id", [PART, PART], F16)
        ones = sb("ones", [PART, HEAD_DIM], F16)
        spread = sb("spread", [PART, PART], F16)
        low_rows = sb("low_rows", [PART, 1], F32)
        p_bias = sb("p_bias", [PART, 1], F32)
        eps = sb("eps", [PART, 1], F32)
        w_scale = sb("w_scale", [PART, 1], F32)
        taps = sb("taps", [PART, PAIRS, CONV_K], F32)
        given = sb("given", [PART, 8], F32)
        stats = sb("stats", [PART, 2, 12], F32)
        mean_var = sb("mean_var", [PART, 2, 2], F32)
        log_var = sb("log_var", [PART, 2], F32)
        rstd = sb("rstd", [PART, 2], F32)

        arg = [ctx.enter_context(nc.psum_tensor(f"arg{i}", [PART, 2, QT], F32)) for i in range(2)]
        sums = ctx.enter_context(nc.psum_tensor("sums", [PART, QT], F32))
        o_acc = ctx.enter_context(nc.psum_tensor("o_acc", [PART, QT], F32))
        proj = [ctx.enter_context(nc.psum_tensor(f"proj{i}", [PART, QT], F32)) for i in range(2)]

        x_in = [buf[:, h * D_MODEL:(h + 1) * D_MODEL] for buf in (b_gate, z_conv, z_attn) for h in range(2)]
        NX = len(x_in)
        UPPER = SEQ - D_MODEL
        wo_hi, wo_lo = xt_hi[:, :, UPPER:SEQ], xt_lo[:, :, UPPER:SEQ]
        mx_hi, mx_lo = ([xt[:, :, i * QT:(i + 1) * QT] for i in range(2)] for xt in (xt_hi, xt_lo))
        rows = [buf[:, h * D_MODEL:(h + 1) * D_MODEL] for h in (1, 0) for buf in (b_gate, z_conv)]
        gain = u_conv[:, 0:D_MODEL]
        bias = u_conv[:, D_MODEL:2 * D_MODEL]
        NR = len(rows)

        consts_done = sem("consts_done")
        rows_done = sem("rows_done")
        taps_loaded = sem("taps_loaded")
        x_loaded = [sem(f"x_loaded{i}") for i in range(NX)]
        xh_done, xl_done = sem("xh_done"), sem("xl_done")
        w_loaded = [sem(f"w_loaded{i}") for i in range(2)]
        w_part = sem("w_part")
        w_ready = sem("w_ready")
        unit_done = sem("unit_done")
        proj_free = [sem(f"proj_free{i}") for i in range(2)]
        hi_done = sem("hi_done")
        z_ready = sem("z_ready")
        min_done, exp1_done, ln_done = sem("min_done"), sem("exp1_done"), sem("ln_done")
        sp_done, sph_done, spl_done = sem("sp_done"), sem("sph_done"), sem("spl_done")
        sums_ready, chi_done, carry_done = sem("sums_ready"), sem("chi_done"), sem("carry_done")
        arg_ready = sem("arg_ready")
        wt_done, wth_done, wtl_done = sem("wt_done"), sem("wth_done"), sem("wtl_done")
        pv_done = sem("pv_done")
        o_taken, omh_done, oml_done = sem("o_taken"), sem("omh_done"), sem("oml_done")
        om_stored = sem("om_stored")
        gate_in = sem("gate_in")
        u_done = sem("u_done")
        silu_done = sem("silu_done")
        y_step, gates_done, mixed, cmh_done, cml_done = (sem(n) for n in
                                                         ("y_step", "gates_done", "mixed", "cmh_done", "cml_done"))
        cm_stored = sem("cm_stored")
        wo_loaded = [sem(f"wo_loaded{i}") for i in range(2)]
        woh_done, wol_done = sem("woh_done"), sem("wol_done")
        affine_loaded = sem("affine_loaded")
        mx_loaded = [sem(f"mx_loaded{i}") for i in range(2)]
        row_loaded = [sem(f"row_loaded{i}") for i in range(NR)]
        mx_later = sem("mx_later")
        sub_ready, row_summed = sem("sub_ready"), sem("row_summed")
        stats_done, var_done, log_done, rstd_done = (sem(n) for n in
                                                     ("stats_done", "var_done", "log_done", "rstd_done"))
        norm_step, row_done = sem("norm_step"), sem("row_done")
        row_stored = [sem(f"row_stored{i}") for i in range(NR)]

        block = ctx.enter_context(nc.Block())

        PV_CREDIT, WTL_CREDIT, O_CREDIT, CML_CREDIT = 2, 1, 1, 2
        STORE_CREDIT = 32
        N_CONSTS, N_ROWS = 8 + 3, 9

        units_mid, steps_mid = schedule(False)
        units_last, steps_last = schedule(True)

        def plan(last):
            return (units_last, steps_last) if last else (units_mid, steps_mid)

        def unit_ends(last):
            _, steps = plan(last)
            ends = [[] for _ in range(NB + 1)]
            for n, mine in enumerate(steps):
                ends[n] += [u for u, i in mine if i == PIECES - 1]
            return ends

        def early_pieces(n, last):
            units, steps = plan(last)
            most = (len(steps[n]) + 1) // 2
            for k, (u, _) in enumerate(steps[n][:most]):
                if not last and u >= len(UNITS_IN) and step_of_end(units[u][1]) + 1 == n:
                    return k
            return most

        def early_ends(n, last):
            mine = plan(last)[1][n]
            return [u for u, i in mine[:early_pieces(n, last)] if i == PIECES - 1] if n < NB else []

        def late_ends(n, last):
            return [u for u in unit_ends(last)[n] if u not in early_ends(n, last)]

        def end_of(last, unit):
            return next(n for n, us in enumerate(unit_ends(last)) if unit in us)

        def split_steps(last):
            out = [[] for _ in range(NB + 1)]
            for j, unit in FREED_BY.items():
                if not last or j <= 4:
                    out[end_of(last, unit)].append(j)
            return out

        def h_unit(tile):
            return UNITS_IN.index((G_H, tile, 1))

        def conv_events(n, last):
            first = end_of(last, LAST_UNIT_ZC) + 1
            starts = [first + 2 * k for k in range(NQT)]
            if last:
                upper = end_of(last, LAST_UNIT_UPPER) + 1
                starts = [upper, max(upper + 2, end_of(last, h_unit(1)) + 1), first, first + 1]
            out = []
            for k, at in enumerate(starts):
                if min(at, NB) == n:
                    out.append(("start", k))
                if min(at + 1, NB) == n:
                    out.append(("finish", k))
            return sorted(out, key=lambda e: (e[1], e[0] == "finish"))

        def out_weights_at(n, last):
            if not last:
                return []
            first = end_of(last, LAST_UNIT_UPPER) + 1
            return [c for c in range(DCH) if first + c == n]

        def rows_at(n, last):
            return [units_last[u][1] for u in unit_ends(last)[n] if u >= len(UNITS_IN) and units_last[u][2] == 1] \
                if last and 0 <= n <= NB else []

        def taken_count(p, u):
            return p * (N_UNITS // 2) + ((N_FIRST + u) // 2 + 1)

        IN_UNITS_DONE = N_FIRST + N_UNITS * (PAIRS - 1) + len(UNITS_IN)

        GROUPS = [G_ZA, G_C, G_H, G_B, G_ZC, G_Q, G_K, G_V, G_ZA, G_C]

        def row_of(r):
            return (NQT - 1 - r // SUB) * SUB + r % SUB

        def load_mixed(eng, m):
            t, i = NQT - 1 - m, m % 2
            eng.wait_ge(unit_done, IN_UNITS_DONE + (0 if m < 2 else 2 * SUB * (m - 1)))
            if m == 3:
                eng.wait_ge(mx_later, 32)
            stored = STORE_CREDIT + 32 * (NQT * (PAIRS - 1) + m + 1)
            eng.wait_ge(om_stored, stored)
            eng.wait_ge(cm_stored, stored)
            for src, dst in ((mix_hi, mx_hi[i]), (mix_lo, mx_lo[i])):
                eng.dma_start(dst, src.rearrange("c p t -> p c t")[:, :, t * QT:(t + 1) * QT])\
                    .then_inc(mx_loaded[i] if m < 2 else mx_later, 16)

        def load_row(eng, r, i):
            eng.dma_start(rows[i], x_rows[row_of(r)]).then_inc(row_loaded[i], 16)

        def load_group(sp_eng, g_index, slot, group, pair):
            sp_eng.dma_start(w_raw[:, slot, :, :].rearrange("p c m -> p (c m)"), w_blocks[group, pair])\
                .then_inc(w_loaded[slot], 16)

        @block.sync
        def _(eng):
            load_group(eng, 0, 0, G_Q, 0)
            for k in range(NX):
                eng.dma_start(x_in[k], x_blocks[NTB - 1 - k]).then_inc(x_loaded[k], 16)
                if k == 1:
                    load_group(eng, 1, 1, G_K, 0)
            eng.wait_ge(w_ready, 1)
            load_group(eng, 2, 0, G_V, 0)
            eng.dma_start(taps[:, :, :], conv_taps_in).then_inc(taps_loaded, 16)
            for k in range(NX, NTB):
                if k == NX + 2:
                    eng.wait_ge(w_ready, 2)
                    load_group(eng, 3, 1, G_ZA, 0)
                eng.wait_ge(xh_done, k - NX + 1)
                eng.wait_ge(xl_done, k - NX + 1)
                eng.dma_start(x_in[k % NX], x_blocks[NTB - 1 - k]).then_inc(x_loaded[k % NX], 16)
            eng.wait_ge(w_ready, 3)
            load_group(eng, 4, 0, G_C, 0)

            def pair_stores(p, last):
                splits = split_steps(last)
                for n in range(NB + 1):
                    for j in splits[n]:
                        if j + 1 <= (4 if last else 9) and j + 1 >= 2:
                            g = 3 + (j + 1)
                            eng.wait_ge(w_ready, p * 8 + (g - 2 + 1))
                            load_group(eng, g, g % 2, GROUPS[j + 1], p + (1 if j + 1 >= 5 else 0))
                    for what, t in conv_events(n, last):
                        if what == "start":
                            continue
                        eng.wait_ge(cml_done, p * NQT + (t + 1 + CML_CREDIT))
                        t = NQT - 1 - t
                        eng.dma_start(mix_hi[p, :, t * QT:(t + 1) * QT], cm_hi[:, :]).then_inc(cm_stored, 16)
                        eng.dma_start(mix_lo[p, :, t * QT:(t + 1) * QT], cm_lo[:, :]).then_inc(cm_stored, 16)
                    if n - 1 in TILE_END:
                        t = TILE_END[n - 1]
                        k = NQT - 1 - t
                        eng.wait_ge(oml_done, p * NQT + (k + 1))
                        eng.dma_start(mix_hi[p + PAIRS, :, t * QT:(t + 1) * QT], om_hi[:, :]).then_inc(om_stored, 16)
                        eng.dma_start(mix_lo[p + PAIRS, :, t * QT:(t + 1) * QT], om_lo[:, :]).then_inc(om_stored, 16)
                    for c in out_weights_at(n, last):
                        if c == 0:
                            eng.wait_ge(w_ready, 3 + 8 * (PAIRS - 1) + 5)
                            load_out_weights(eng, 0)
                            load_out_weights(eng, 1)
                        if c + 2 < DCH:
                            eng.wait_ge(wol_done, c + 1)
                            load_out_weights(eng, c + 2)
                    if last and ("finish", 1) in conv_events(n, last):
                        eng.wait_ge(cm_stored, STORE_CREDIT + 32 * (NQT * (PAIRS - 1) + 2))
                        load_row(eng, 0, 0)
                        load_row(eng, 1, 1)
                    if last and ("finish", NQT - 1) in conv_events(n, last):
                        eng.wait_ge(cm_stored, STORE_CREDIT + 32 * NQT * PAIRS)
                        load_row(eng, 2, 2)
                        load_row(eng, 3, 3)
                        for name, dst in ((ln_gain, gain), (ln_bias, bias)):
                            eng.dma_start(dst, name[0:1, :].broadcast_to([PART, D_MODEL])).then_inc(affine_loaded, 16)
                    for m in range(NQT):
                        finish = next(s for s in range(NB + 1) if ("finish", m) in conv_events(s, last))
                        if last and n == max(finish, step_of_end(NQT - 1 - m) + 1, end_of(last, LAST_UNIT_ZC) + 1):
                            load_mixed(eng, m)
                    for r in rows_at(n - 1, last):
                        store_row(eng, r)

            def load_out_weights(eng, c):
                eng.dma_start(w_raw[:, c % 2, :, :].rearrange("p c m -> p (c m)"), wo_rows[c])\
                    .then_inc(wo_loaded[c % 2], 16)

            def store_row(eng, r):
                eng.wait_ge(row_done, r + 1)
                eng.dma_start(out_rows[row_of(r)], rows[r % NR]).then_inc(row_stored[r % NR], 16)
                if r >= 1 and r - 1 + NR < NTB:
                    eng.wait_ge(row_stored[(r - 1) % NR], 16 * ((r - 1) // NR + 1))
                    load_row(eng, r - 1 + NR, (r - 1) % NR)

            for p in range(PAIRS):
                pair_stores(p, p == PAIRS - 1)

            for r in rows_at(NB, True):
                store_row(eng, r)
            for r in range(ROWS_EARLY, NTB):
                store_row(eng, r)
            for i in range(NR):
                eng.wait_ge(row_stored[i], 16 * (NTB // NR))

        @block.tensor
        def _(pe):
            mm = nc.tensor.matmul

            def unit_products(unit):
                group, t, slot = unit
                prods = []
                if group == G_OUT:
                    r, half = t, slot
                    i, tok = r // SUB, slice(r % SUB * PART, (r % SUB + 1) * PART)
                    for c in range(DCH):
                        for a, b in ((mx_hi, wo_hi), (mx_hi, wo_lo), (mx_lo, wo_hi)):
                            prods.append((slice(0, QT), a[i][:, c, tok], b[:, c, half * QT:(half + 1) * QT],
                                          c == 0 and a is mx_hi and b is wo_hi,
                                          c == DCH - 1 and a is mx_lo))
                elif group == G_V:
                    for s in range(SUB):
                        tok = slice(t * QT + s * PART, t * QT + (s + 1) * PART)
                        for d in range(DCH):
                            for a, b in ((xt_hi, w_hi), (xt_hi, w_lo), (xt_lo, w_hi)):
                                prods.append((slice(s * PART, (s + 1) * PART), a[:, d, tok], b[:, slot, d, :],
                                              d == 0 and a is xt_hi and b is w_hi,
                                              d == DCH - 1 and a is xt_lo))
                else:
                    tok = slice(t * QT, (t + 1) * QT)
                    for d in range(DCH):
                        for a, b in ((w_hi, xt_hi), (w_hi, xt_lo), (w_lo, xt_hi)):
                            prods.append((slice(0, QT), a[:, slot, d, :], b[:, d, tok],
                                          d == 0 and a is w_hi and b is xt_hi,
                                          d == DCH - 1 and a is w_lo))
                return prods

            def unit_piece(p, index, unit, piece, wait_weights):
                prods = unit_products(unit)
                size = len(prods) // PIECES
                bank = (N_FIRST + index) % 2
                if piece == 0:
                    if wait_weights is not None:
                        pe.wait_ge(w_ready, wait_weights)
                    if unit[0] == G_OUT and unit[2] == 0 and unit[1] % SUB == 0:
                        pe.wait_ge(wol_done, DCH)
                        pe.wait_ge(mx_loaded[unit[1] // SUB], 32)
                    uses = (N_FIRST + index) // 2
                    if index >= 0 or uses > 0:
                        pe.wait_ge(proj_free[bank], p * (N_UNITS // 2) + uses)
                for cols, lhs, rhs, start, stop in prods[piece * size:(piece + 1) * size]:
                    last = mm(proj[bank][:, cols], lhs, rhs, start=start, stop=stop)
                if piece == PIECES - 1:
                    last.then_inc(unit_done, 1)

            pe.wait_ge(consts_done, N_CONSTS)
            pe.wait_ge(rows_done, N_ROWS)
            for tile in range(NQT):
                if tile < NQT - 1:
                    pe.wait_ge(xl_done, (tile + 1) * SUB)
                    pe.wait_ge(xh_done, (tile + 1) * SUB)
                    for g in range(3):
                        i = 3 * tile + g
                        for piece in range(PIECES):
                            unit_piece(0, i - N_FIRST, UNITS_FIRST[i], piece, g + 1 if tile == 0 else None)
            pe.wait_ge(xl_done, NTB)
            pe.wait_ge(xh_done, NTB)

            def pair_products(p, last, first_scores=False):
                units, steps = plan(last)

                def pieces(todo):
                    for u, i in todo:
                        j = None if units[u][0] == G_OUT else FIRST_OF_GROUP.get(u)
                        weights = None if j is None else p * 8 + (3 + j + 1)
                        unit_piece(p, u, units[u], i, weights)

                def scores(n):
                    t, b, c0 = BLOCKS[n % NB]
                    if n >= 2:
                        pe.wait_ge(wt_done, p * NB + (n - 2 + 1))
                    if t == NQT - 1 and b % SUB == SUB - 1:
                        for bank in range(2):
                            units_before = 3 * (NQT - b // SUB) + N_UNITS * (n // NB)
                            pe.wait_ge(proj_free[bank], p * (N_UNITS // 2) + (units_before + 1 - bank) // 2)
                    keys = slice(b * PART, (b + 1) * PART)
                    cols = slice(t * QT + c0, (t + 1) * QT)
                    diagonal = b >= SUB * t
                    for i, (a, c) in enumerate(((k_hi, q_hi), (k_hi, q_lo), (k_lo, q_hi))):
                        for h in range(2):
                            rows_h = slice(h * HEAD_DIM, (h + 1) * HEAD_DIM)
                            last_mm = mm(arg[n % 2][:, h, c0:QT], a[rows_h, keys], c[rows_h, cols],
                                         start=(i == 0), stop=(i == 2), skip_group_check=True)
                    if diagonal:
                        for h in range(2):
                            last_mm = mm(arg[n % 2][:, h, c0:c0 + PART], root_id[:, :], future[:, :],
                                         start=False, stop=True, skip_group_check=True)
                    last_mm.then_inc(z_ready, 1)

                def carried(n):
                    t, b, c0 = BLOCKS[n]
                    if b == SUB * (t + 1) - 1:
                        return
                    pe.wait_ge(carry_done, p * SUMS + SUMS_BEFORE[n])
                    c1 = BLOCKS[n - 1][2]
                    for h in range(2):
                        rows_h = slice(h * HEAD_DIM, (h + 1) * HEAD_DIM)
                        mm(arg[n % 2][:, h, c1:QT], spread[rows_h, :], carry[rows_h, c1:QT],
                           start=False, stop=True, skip_group_check=True)

                def sums_within(n):
                    t, b, c0 = BLOCKS[n]
                    pe.wait_ge(spl_done, p * NB + (n + 1))
                    carried(n)
                    first = b == SUB * (t + 1) - 1
                    if b > 0:
                        for part in (sp_hi, sp_lo):
                            for h in range(2):
                                last_mm = mm(sums[h * HEAD_DIM:(h + 1) * HEAD_DIM, c0:QT], ones[:, :],
                                             part[:, n % 2, h, c0:QT], start=(first and part is sp_hi), stop=True,
                                             skip_group_check=True)
                        last_mm.then_inc(sums_ready, 1)
                    for part in (sp_hi, sp_lo):
                        for h in range(2):
                            last_mm = mm(arg[n % 2][:, h, c0:QT], tri[:, :], part[:, n % 2, h, c0:QT],
                                         start=False, stop=True, skip_group_check=True)
                    last_mm.then_inc(arg_ready, 1)

                def values(n):
                    t, b, c0 = BLOCKS[n]
                    pe.wait_ge(wtl_done, p * NB + (n + 1 + WTL_CREDIT))
                    first = b == SUB * (t + 1) - 1
                    if first:
                        pe.wait_ge(o_taken, p * NQT + (NQT - 1 - t + O_CREDIT))
                    for i, (a, c) in enumerate(((v_hi, wt_hi), (v_hi, wt_lo), (v_lo, wt_hi))):
                        for h in range(2):
                            cols_h = slice(h * HEAD_DIM, (h + 1) * HEAD_DIM)
                            last_mm = mm(o_acc[cols_h, c0:QT], a[:, b, cols_h], c[:, n % 2, h, c0:QT],
                                         start=(first and i == 0), stop=(i == 2), skip_group_check=True)
                    last_mm.then_inc(pv_done, 1)

                if first_scores:
                    scores(0)
                    scores(1)
                    return
                for n in range(NB):
                    early = early_pieces(n, last)
                    sums_within(n)
                    pieces(steps[n][:early])
                    if not last or n + 2 < NB:
                        scores(n + 2)
                    if n >= 1:
                        values(n - 1)
                    pieces(steps[n][early:])
                values(NB - 1)
                pieces(steps[NB])

            pair_products(0, False, first_scores=True)
            with pe.Fori(0, PAIRS - 1) as p:
                pair_products(p, False)
            pair_products(PAIRS - 1, True)

            with pe.Fori(0, 2) as tile:
                pe.wait_ge(mx_later, tile * 32 + 32)
                for s in range(SUB):
                    pe.wait_ge(row_summed, tile * SUB + (s - 2 + 1 + 2))
                    for half in range(2):
                        for c in range(DCH):
                            for m, (a, b) in enumerate(((xt_hi, wo_hi), (xt_hi, wo_lo), (xt_lo, wo_hi))):
                                last = mm(arg[s % 2][:, half, :], a[:, c, bass.ds(tile * QT + s * PART, PART)],
                                          b[:, c, half * QT:(half + 1) * QT],
                                          start=(c == 0 and m == 0), stop=(c == DCH - 1 and m == 2))
                    last.then_inc(sub_ready, 1)

        def high_place(unit):
            group, t, _ = unit
            tok = slice(t * QT, (t + 1) * QT)
            if group == G_V:
                return (v_hi[:, t * SUB:(t + 1) * SUB, :].rearrange("p s c -> p (s c)"),
                        v_lo[:, t * SUB:(t + 1) * SUB, :].rearrange("p s c -> p (s c)"))
            return (q_hi[:, tok], q_lo[:, tok]) if group == G_Q else (k_hi[:, tok], k_lo[:, tok])

        def first_hi(act, i):
            act.wait_ge(unit_done, i + 1)
            nc.scalar.activation(high_place(UNITS_FIRST[i])[0], proj[i % 2][:, :], ACT.Copy, scale=PROJ_SCALE)\
                .then_inc(hi_done, 1)

        def hi_count(u):
            return u + 1 if u < 3 else 3 + (u - len(UNITS_IN)) + 1

        def take_unit(act, p, u, unit, last):
            group, t, _ = unit
            bank = (N_FIRST + u) % 2
            tok = slice(t * QT, (t + 1) * QT)
            if group in (G_H, G_OUT):
                return
            act.wait_ge(unit_done, p * N_UNITS + (N_FIRST + u + 1))
            if group in (G_Q, G_K, G_V):
                nc.scalar.activation(high_place(unit)[0], proj[bank][:, :], ACT.Copy, scale=PROJ_SCALE)\
                    .then_inc(hi_done, 1)
                return
            dst = {G_ZA: z_attn[:, tok], G_B: b_gate[:, tok], G_ZC: z_conv[:, tok],
                   G_C: u_conv[:, CONV_K - 1 + t * QT:CONV_K - 1 + (t + 1) * QT]}[group]
            nc.scalar.activation(dst, proj[bank][:, :], ACT.Copy, scale=PROJ_SCALE).then_inc(proj_free[bank], 1)
            halves = last and group == G_ZC
            if u in (LAST_UNIT_ZA, LAST_UNIT_ZC) or (halves and u == LAST_UNIT_UPPER):
                gate = z_attn if group == G_ZA else z_conv
                part = slice(0, SEQ) if not halves else slice(UPPER, SEQ) if u == LAST_UNIT_UPPER else slice(0, UPPER)
                for bk, back in ((bank, 0), (1 - bank, 1)):
                    act.wait_ge(proj_free[bk], taken_count(p, u - back))
                nc.scalar.activation(gate[:, part], gate[:, part], ACT.Silu).then_inc(silu_done, 1)
                nc.scalar.preload_act_table_set(TABLES)

        @block.scalar
        def _(act):
            act.wait_ge(consts_done, N_CONSTS)
            nc.scalar.preload_act_table_set(TABLES)
            for k in range(NTB):
                act.wait_ge(x_loaded[k % NX], 16 * (k // NX + 1))
                blk = NTB - 1 - k
                nc.scalar.activation(xt_hi[:, :, blk * PART:(blk + 1) * PART],
                                     x_in[k % NX].rearrange("p (c t) -> p c t", t=PART),
                                     ACT.Copy, scale=X_SCALE).then_inc(xh_done, 1)
                if k >= SUB and k % SUB < 3:
                    first_hi(act, 3 * (k // SUB - 1) + k % SUB)

            def deviation(act, i, count):
                act.wait_ge(var_done, count)
                nc.scalar.activation(log_var[:, i % 2:i % 2 + 1], mean_var[:, i % 2, 1:2], ACT.Ln,
                                     bias=eps[:, :], scale=1.0 / W_SCALE ** 2).then_inc(log_done, 1)
                act.wait_ge(log_done, count)
                nc.scalar.activation(rstd[:, i % 2:i % 2 + 1], log_var[:, i % 2:i % 2 + 1], ACT.Exp,
                                     scale=-0.5).then_inc(rstd_done, 1)

            def pair_activations(p, last, first_blocks=False):
                units, _ = plan(last)

                def softplus_terms(n):
                    e = sp[:, n % 2, :, BLOCKS[n % NB][2]:QT]
                    act.wait_ge(min_done, p * NB + (n + 1))
                    nc.scalar.activation(e, e, ACT.Exp).then_inc(exp1_done, 1)
                    act.wait_ge(exp1_done, p * NB + (n + 1))
                    nc.scalar.activation(e, e, ACT.Ln, bias=1.0).then_inc(ln_done, 1)

                def softplus_high(n):
                    c0 = BLOCKS[n % NB][2]
                    act.wait_ge(sp_done, p * NB + (n + 1))
                    nc.scalar.activation(sp_hi[:, n % 2, :, c0:QT], sp[:, n % 2, :, c0:QT], ACT.Copy)\
                        .then_inc(sph_done, 1)

                if first_blocks:
                    for n in range(2):
                        softplus_terms(n)
                    softplus_high(0)
                    return
                for n in range(NB + 1):
                    more = n < NB and (not last or n + 2 < NB)
                    if n < NB:
                        c0 = BLOCKS[n][2]
                        act.wait_ge(arg_ready, p * NB + (n + 1))
                        act.wait_ge(wtl_done, p * NB + (n + WTL_CREDIT))
                        nc.scalar.activation(wt[:, :, c0:QT], arg[n % 2][:, :, c0:QT], ACT.Exp,
                                             bias=p_bias[:, :], scale=1.0 / ROOT).then_inc(wt_done, 1)
                        if not last or n + 1 < NB:
                            softplus_high(n + 1)
                        act.wait_ge(wt_done, p * NB + (n + 1))
                        act.wait_ge(pv_done, p * NB + (n - 2 + 1 + PV_CREDIT))
                        nc.scalar.activation(wt_hi[:, n % 2, :, c0:QT], wt[:, :, c0:QT], ACT.Copy)\
                            .then_inc(wth_done, 1)
                    for u in early_ends(n, last):
                        take_unit(act, p, u, units[u], last)
                    if more:
                        softplus_terms(n + 2)
                    for u in late_ends(n, last):
                        take_unit(act, p, u, units[u], last)
                    for c in out_weights_at(n, last):
                        act.wait_ge(wo_loaded[c % 2], 16 * (c // 2 + 1))
                        if c == 0:
                            act.wait_ge(unit_done, N_FIRST + N_UNITS * (PAIRS - 1) + LAST_UNIT_UPPER + 1)
                        nc.scalar.activation(wo_hi[:, c, :], w_raw[:, c % 2, :, :].rearrange("p c m -> p (c m)"),
                                             ACT.Copy, scale=W_SCALE).then_inc(woh_done, 1)
                    for r in rows_at(n - 1, last):
                        deviation(act, r % NR, r + 1)

            pair_activations(0, False, first_blocks=True)
            with act.Fori(0, PAIRS - 1) as p:
                pair_activations(p, False)
            pair_activations(PAIRS - 1, True)

            for r in rows_at(NB, True):
                deviation(act, r % NR, r + 1)
            with act.Fori(0, 2) as tile:
                for s in range(SUB):
                    deviation(act, s, tile * SUB + (ROWS_EARLY + s + 1))

        def first_low(dve, i):
            dve.wait_ge(hi_done, i + 1)
            hi, lo = high_place(UNITS_FIRST[i])
            nc.vector.scalar_tensor_tensor(out=lo, in0=proj[i % 2][:, :], scalar=PROJ_SCALE, in1=hi, op0=ALU.mult,
                                           op1=ALU.subtract).then_inc(proj_free[i % 2], 1)

        @block.vector
        def _(dve):
            stt = nc.vector.scalar_tensor_tensor

            nc.vector.memset(spread[:, :], 0.0).then_inc(rows_done, 1)
            dve.wait_ge(rows_done, 1)
            for i in range(4):
                nc.vector.memset(spread[32 * i:32 * i + 1, :], -ROOT).then_inc(rows_done, 1)
                nc.vector.memset(low_rows[32 * i:32 * i + 32, :], float(i % 2)).then_inc(rows_done, 1)
            dve.wait_ge(consts_done, N_CONSTS)
            dve.wait_ge(rows_done, N_ROWS)
            dve.wait_ge(taps_loaded, 16)
            for k in range(NTB):
                dve.wait_ge(xh_done, k + 1)
                blk = NTB - 1 - k
                cols = slice(blk * PART, (blk + 1) * PART)
                stt(out=xt_lo[:, :, cols], in0=x_in[k % NX].rearrange("p (c t) -> p c t", t=PART),
                    scalar=X_SCALE, in1=xt_hi[:, :, cols], op0=ALU.mult, op1=ALU.subtract).then_inc(xl_done, 1)
                if k >= SUB and k % SUB < 3:
                    first_low(dve, 3 * (k // SUB - 1) + k % SUB)

            def row_statistics(i, count):
                for half in range(2):
                    nc.vector.bn_stats(stats[:, i % 2, 6 * half:6 * half + 6], rows[i][:, half * QT:(half + 1) * QT])\
                        .then_inc(stats_done, 1)
                dve.wait_ge(stats_done, count(2))
                nc.vector.memset(given[:, 0:1], 0.0)
                nc.vector.bn_aggr(mean_var[:, i % 2, :], stats[:, i % 2, :]).then_inc(var_done, 1)

            def normalise(i, before):
                if i == 0:
                    dve.wait_ge(affine_loaded, 32)
                dve.wait_ge(var_done, before(1) + 1)
                dve.wait_ge(rstd_done, before(1) + 1)
                nc.vector.tensor_scalar(rows[i], rows[i], mean_var[:, i % 2, 0:1], rstd[:, i % 2:i % 2 + 1],
                                        ALU.subtract, ALU.mult).then_inc(norm_step, 1)
                dve.wait_ge(norm_step, before(2) + 1)
                stt(out=rows[i], in0=rows[i], scalar=1.0 / W_SCALE, in1=gain, op0=ALU.mult, op1=ALU.mult)\
                    .then_inc(norm_step, 1)
                dve.wait_ge(norm_step, before(2) + 2)
                nc.vector.tensor_tensor(rows[i], rows[i], bias, ALU.add).then_inc(row_done, 1)

            def pair_vectors(p, last, first_blocks=False):
                units, _ = plan(last)

                def clamp(n):
                    c0 = BLOCKS[n % NB][2]
                    dve.wait_ge(z_ready, p * NB + (n + 1))
                    nc.vector.tensor_scalar(sp[:, n % 2, :, c0:QT], arg[n % 2][:, :, c0:QT], 1.0 / ROOT, EXP_CLAMP,
                                            ALU.mult, ALU.min).then_inc(min_done, 1)

                def softplus_guard(n):
                    c0 = BLOCKS[n % NB][2]
                    dve.wait_ge(ln_done, p * NB + (n + 1))
                    stt(out=sp[:, n % 2, :, c0:QT], in0=arg[n % 2][:, :, c0:QT], scalar=1.0 / ROOT,
                        in1=sp[:, n % 2, :, c0:QT], op0=ALU.mult, op1=ALU.max).then_inc(sp_done, 1)

                def softplus_low(n):
                    c0 = BLOCKS[n % NB][2]
                    dve.wait_ge(sph_done, p * NB + (n + 1))
                    nc.vector.tensor_tensor(sp_lo[:, n % 2, :, c0:QT], sp[:, n % 2, :, c0:QT], sp_hi[:, n % 2, :, c0:QT],
                                            ALU.subtract).then_inc(spl_done, 1)

                def split_carry(n):
                    _, b, c0 = BLOCKS[n]
                    if b == 0:
                        return
                    dve.wait_ge(sums_ready, p * SUMS + (SUMS_BEFORE[n] + 1))
                    nc.vector.tensor_scalar(carry_hi[:, c0:QT], sums[:, c0:QT], CUT, low_rows[:, :],
                                            ALU.min, ALU.mult).then_inc(chi_done, 1)
                    dve.wait_ge(chi_done, p * SUMS + (SUMS_BEFORE[n] + 1))
                    stt(out=carry[:, c0:QT], in0=sums[:, c0:QT], scalar=CUT, in1=carry_hi[:, c0:QT],
                        op0=ALU.min, op1=ALU.subtract).then_inc(carry_done, 1)

                def take(u):
                    group, t, _ = units[u]
                    bank = (N_FIRST + u) % 2
                    if group == G_H:
                        dve.wait_ge(unit_done, p * N_UNITS + (N_FIRST + u + 1))
                        dve.wait_ge(proj_free[1 - bank], taken_count(p, u - 1))
                        at = u_conv[:, CONV_K - 1 + t * QT:CONV_K - 1 + (t + 1) * QT]
                        stt(out=at, in0=proj[bank][:, :], scalar=PROJ_SCALE, in1=at, op0=ALU.mult, op1=ALU.mult)\
                            .then_inc(proj_free[bank], 1)
                    elif group == G_OUT:
                        r, half = units[u][1:]
                        cols = slice(half * QT, (half + 1) * QT)
                        dve.wait_ge(unit_done, p * N_UNITS + (N_FIRST + u + 1))
                        if half == 0:
                            dve.wait_ge(row_loaded[r % NR], 16 * (r // NR + 1))
                        stt(out=rows[r % NR][:, cols], in0=rows[r % NR][:, cols], scalar=ALPHA * W_SCALE,
                            in1=proj[bank][:, :], op0=ALU.mult, op1=ALU.add).then_inc(proj_free[bank], 1)
                        if half == 1:
                            dve.wait_ge(proj_free[1 - bank], taken_count(p, u - 1))
                            dve.wait_ge(proj_free[bank], taken_count(p, u))
                            row_statistics(r % NR, lambda per: per * (r + 1))
                    elif group in (G_Q, G_K, G_V):
                        dve.wait_ge(hi_done, p * 12 + (9 + hi_count(u)))
                        hi, lo = high_place(units[u])
                        stt(out=lo, in0=proj[bank][:, :], scalar=PROJ_SCALE, in1=hi, op0=ALU.mult,
                            op1=ALU.subtract).then_inc(proj_free[bank], 1)

                def conv_taps(t):
                    near = h_unit(max(0, NQT - 2 - t))
                    dve.wait_ge(proj_free[(N_FIRST + near) % 2], taken_count(p, near))
                    dve.wait_ge(cml_done, p * NQT + (t - 1 + CML_CREDIT))
                    y = y_conv[:, t % 2, :]
                    base = (NQT - 1 - t) * QT
                    nc.vector.tensor_scalar(y, u_conv[:, base + 2:base + 2 + QT], taps[:, bass.ds(p, 1), 2],
                                            None, ALU.mult).then_inc(y_step, 1)
                    for j in (1, 0):
                        dve.wait_ge(y_step, p * (3 * NQT) + (3 * t + 2 - j))
                        stt(out=y, in0=u_conv[:, base + j:base + j + QT], scalar=taps[:, bass.ds(p, 1), j],
                            in1=y, op0=ALU.mult, op1=ALU.add).then_inc(y_step, 1)

                def conv_high(t):
                    dve.wait_ge(mixed, p * NQT + (t + 1))
                    dve.wait_ge(cm_stored, p * (32 * NQT) + (32 * t + STORE_CREDIT))
                    nc.vector.tensor_copy(cm_hi[:, :], y_conv[:, t % 2, :]).then_inc(cmh_done, 1)

                def take_output(t):
                    k = NQT - 1 - t
                    n = next(m for m, tt in TILE_END.items() if tt == t)
                    dve.wait_ge(pv_done, p * NB + (n + 1 + PV_CREDIT))
                    if k == 0:
                        dve.wait_ge(silu_done, p * 2 + 1)
                    dve.wait_ge(om_stored, p * (32 * NQT) + (32 * k + STORE_CREDIT))
                    stt(out=o_gated[:, :], in0=o_acc[:, :], scalar=1.0 / P_SCALE,
                        in1=z_attn[:, t * QT:(t + 1) * QT], op0=ALU.mult, op1=ALU.mult).then_inc(o_taken, 1)
                    dve.wait_ge(o_taken, p * NQT + (k + 1 + O_CREDIT))
                    nc.vector.tensor_copy(om_hi[:, :], o_gated[:, :]).then_inc(omh_done, 1)

                if first_blocks:
                    for step in (clamp, softplus_guard):
                        for n in range(2):
                            step(n)
                    softplus_low(0)
                    return
                for n in range(NB + 1):
                    more = n < NB and (not last or n + 2 < NB)
                    if n < NB:
                        split_carry(n)
                    if more:
                        clamp(n + 2)
                    if n < NB and (not last or n + 1 < NB):
                        softplus_low(n + 1)
                    for u in early_ends(n, last):
                        take(u)
                    if more:
                        softplus_guard(n + 2)
                    if n - 1 in TILE_END:
                        take_output(TILE_END[n - 1])
                    for u in late_ends(n, last):
                        take(u)
                    for what, t in conv_events(n, last):
                        (conv_taps if what == "start" else conv_high)(t)
                    for c in out_weights_at(n, last):
                        dve.wait_ge(woh_done, c + 1)
                        stt(out=wo_lo[:, c, :], in0=w_raw[:, c % 2, :, :].rearrange("p c m -> p (c m)"),
                            scalar=W_SCALE, in1=wo_hi[:, c, :], op0=ALU.mult, op1=ALU.subtract).then_inc(wol_done, 1)
                    for r in rows_at(n - 1, last):
                        normalise(r % NR, lambda per, r=r: per * r)

            pair_vectors(0, False, first_blocks=True)
            with dve.Fori(0, PAIRS - 1) as p:
                pair_vectors(p, False)
            pair_vectors(PAIRS - 1, True)

            for r in rows_at(NB, True):
                normalise(r % NR, lambda per, r=r: per * r)
            with dve.Fori(0, 2) as tile:
                for s in range(SUB):
                    dve.wait_ge(sub_ready, tile * SUB + (s + 1))
                    dve.wait_ge(row_loaded[s], tile * 16 + 16 * (ROWS_EARLY // NR + 1))
                    stt(out=rows[s], in0=rows[s], scalar=ALPHA * W_SCALE,
                        in1=arg[s % 2][:, :, :].rearrange("p h n -> p (h n)"), op0=ALU.mult, op1=ALU.add)\
                        .then_inc(row_summed, 1)
                    dve.wait_ge(row_summed, tile * SUB + (s + 1 + 2))
                    row_statistics(s, lambda per: tile * (SUB * per) + per * (ROWS_EARLY + s + 1))
                    normalise(s, lambda per: tile * (SUB * per) + per * (ROWS_EARLY + s))

        @block.gpsimd
        def _(pool):
            below = dict(pattern=[[-1, PART]], base=0, channel_multiplier=1)
            credits = [(pv_done, PV_CREDIT), (wtl_done, WTL_CREDIT), (o_taken, O_CREDIT),
                       (cml_done, CML_CREDIT), (om_stored, STORE_CREDIT), (cm_stored, STORE_CREDIT), (row_summed, 2)]
            for i, (what, n) in enumerate(credits):
                nc.gpsimd.memset(given[:, i:i + 1], 0.0).then_inc(what, n)
            fills = [(tri[:, :], -ROOT), (future[:, :], -CUT), (root_id[:, :], 0.0),
                     (ones[:, :], 1.0), (p_bias[:, :], math.log(P_SCALE)),
                     (eps[:, :], LN_EPS), (w_scale[:, :], W_SCALE), (u_conv[:, 0:CONV_K - 1], 0.0)]
            for dst, value in fills:
                nc.gpsimd.memset(dst, value).then_inc(consts_done, 1)
            pool.wait_ge(consts_done, len(fills))
            for dst in (tri, future):
                nc.gpsimd.affine_select(out=dst[:, :], in_=dst[:, :], compare_op=ALU.is_ge, fill=0.0, **below)\
                    .then_inc(consts_done, 1)
            for dst, value in ((root_id, ROOT),):
                nc.gpsimd.affine_select(out=dst[:, :], in_=dst[:, :], compare_op=ALU.not_equal, fill=value, **below)\
                    .then_inc(consts_done, 1)

            def split_weights(slot, raw, loaded, ready_before):
                pool.wait_ge(w_loaded[raw], loaded)
                flat = lambda a: a.rearrange("p c m -> p (c m)")
                w = flat(w_raw[:, raw, :, :])
                hi, lo = flat(w_hi[:, slot, :, :]), flat(w_lo[:, slot, :, :])
                nc.gpsimd.tensor_tensor(hi, w, w_scale[:, 0:1].broadcast_to([PART, D_MODEL]), ALU.mult)\
                    .then_inc(w_part, 1)
                nc.gpsimd.tensor_scalar(w, w, W_SCALE, 1.0, ALU.mult, ALU.mult).then_inc(w_part, 1)
                pool.wait_ge(w_part, ready_before)
                nc.gpsimd.tensor_tensor(lo, w, hi, ALU.subtract).then_inc(w_ready, 1)

            for g in range(4):
                split_weights(g, g % 2, 16 * (g // 2 + 1), 2 * (g + 1))

            def pair_pool(p, last):
                splits = split_steps(last)
                for n in range(NB + 1):
                    if n < NB:
                        c0 = BLOCKS[n][2]
                        pool.wait_ge(wth_done, p * NB + (n + 1))
                        nc.gpsimd.tensor_tensor(wt_lo[:, n % 2, :, c0:QT], wt[:, :, c0:QT],
                                                wt_hi[:, n % 2, :, c0:QT], ALU.subtract).then_inc(wtl_done, 1)
                    for j in splits[n]:
                        g = 3 + j
                        unit = FREED_BY[j]
                        pool.wait_ge(unit_done, p * N_UNITS + (N_FIRST + unit + 1))
                        split_weights(g % 4, g % 2, p * 64 + 16 * (g // 2 + 1), p * 16 + 2 * (g + 1))
                    for what, t in conv_events(n, last):
                        tok = slice((NQT - 1 - t) * QT, (NQT - t) * QT)
                        if what == "start":
                            pool.wait_ge(silu_done, p * 2 + (3 if last and t >= 2 else 2))
                            nc.gpsimd.tensor_tensor(b_gate[:, tok], b_gate[:, tok], z_conv[:, tok], ALU.mult)\
                                .then_inc(gates_done, 1)
                            pool.wait_ge(gates_done, p * NQT + (t + 1))
                            pool.wait_ge(y_step, p * (3 * NQT) + 3 * (t + 1))
                            nc.gpsimd.tensor_tensor(y_conv[:, t % 2, :], y_conv[:, t % 2, :], b_gate[:, tok], ALU.mult)\
                                .then_inc(mixed, 1)
                        else:
                            pool.wait_ge(cmh_done, p * NQT + (t + 1))
                            nc.gpsimd.tensor_tensor(cm_lo[:, :], y_conv[:, t % 2, :], cm_hi[:, :], ALU.subtract)\
                                .then_inc(cml_done, 1)
                    if n - 1 in TILE_END:
                        k = NQT - 1 - TILE_END[n - 1]
                        pool.wait_ge(omh_done, p * NQT + (k + 1))
                        nc.gpsimd.tensor_tensor(om_lo[:, :], o_gated[:, :], om_hi[:, :], ALU.subtract)\
                            .then_inc(oml_done, 1)

            with pool.Fori(0, PAIRS - 1) as p:
                pair_pool(p, False)
            pair_pool(PAIRS - 1, True)


_OUT = ((1, SEQ, D_MODEL), "float32")


def kernel(**inputs):
    import numpy as _np
    import concourse.bacc as _bacc
    from concourse import mybir as _mybir
    from concourse.bass_utils import run_bass_kernel_spmd as _run

    nc = _bacc.Bacc("TRN2", target_bir_lowering=False, num_devices=1)
    arrays, args = {}, []
    laid_out = {
        "x": inputs["x"],
        "x_blocks": inputs["x"][0].reshape(NTB, PART, DCH, PART).transpose(0, 3, 2, 1).reshape(NTB, PART, D_MODEL),
        "w_blocks": inputs["w_in"][0].reshape(DCH, PART, 8, PAIRS, PART).transpose(2, 3, 1, 0, 4)
                    .reshape(8, PAIRS, PART, D_MODEL),
        "conv_taps": inputs["conv_w"][0].reshape(CONV_K, PAIRS, PART).transpose(2, 1, 0),
        "w_out": inputs["w_out"], "ln_gain": inputs["ln_gain"], "ln_bias": inputs["ln_bias"],
    }
    for name, laid in laid_out.items():
        a = _np.ascontiguousarray(laid)
        arrays[f"in_{name}_dram"] = a
        args.append(nc.dram_tensor(f"in_{name}_dram", a.shape, _mybir.dt.from_np(a.dtype), kind="ExternalInput").ap())
    shape, dtype = _OUT
    args.append(nc.dram_tensor("out_0_dram", shape, _mybir.dt.from_np(_np.dtype(dtype)), kind="ExternalOutput").ap())
    layer_program(nc, *args)
    r = _run(nc, [arrays], core_ids=[0])
    return r.results[0]["out_0_dram"]
```

```python
import math

import concourse.bass as bass
from concourse import mybir
from contextlib import ExitStack

F32 = mybir.dt.float32
F16 = mybir.dt.float16
ALU = mybir.AluOpType
ACT = mybir.ActivationFunctionType

SEQ, D_MODEL, PROJ = 2048, 1024, 4096
CONV_W = ATTN_W = 512
HEAD_DIM = 64
CONV_K = 3
LN_EPS = 1e-5
ALPHA = 2.0 ** 0.25
PART = 128
DCH = D_MODEL // PART
QT = 512
NQT = SEQ // QT
SUB = QT // PART
NTB = SEQ // PART
PAIRS = ATTN_W // PART
CUT = 60000.0
ROOT = 8.0
X_SCALE, W_SCALE, P_SCALE = 16.0, 512.0, 1024.0
PROJ_SCALE = 1.0 / (X_SCALE * W_SCALE)
EXP_CLAMP = 40.0
TABLES = "natural_log_exp_and_others"

G_B, G_C, G_H, G_ZC, G_Q, G_K, G_V, G_ZA = range(8)


def blocks_of_pair():
    out = []
    for t in reversed(range(NQT)):
        for b in reversed(range(SUB * (t + 1))):
            out.append((t, b, PART * max(0, b - SUB * t)))
    return out


BLOCKS = blocks_of_pair()
NB = len(BLOCKS)
SUMS_BEFORE = [sum(1 for _, b, _ in BLOCKS[:n] if b > 0) for n in range(NB + 1)]
SUMS = SUMS_BEFORE[NB]
TILE_END = {n: t for n, (t, b, _) in enumerate(BLOCKS) if b == 0}

UNITS_IN = [(G_V, 0, 0), (G_Q, 0, 1), (G_K, 0, 2)]
UNITS_IN += [(G_ZA, t, 3) for t in range(NQT)]
UNITS_IN += [(_g, t, _s) for t in reversed(range(NQT)) for _g, _s in ((G_C, 0), (G_H, 1), (G_B, 2), (G_ZC, 3))]
UNITS_NEXT = [(g, t, s) for t in (3, 2, 1) for g, s in ((G_V, 0), (G_Q, 1), (G_K, 2))]
UNITS_FIRST = UNITS_NEXT
N_FIRST, N_UNITS = len(UNITS_FIRST), len(UNITS_IN) + len(UNITS_NEXT)
G_OUT = 8
ROWS_EARLY = 2 * SUB
UNITS_OUT = [(G_OUT, r, h) for r in range(ROWS_EARLY) for h in range(2)]
PIECES = 8
STEP_COST, FIRST_COST, TAIL_COST = 350, 500, 250
LAST_UNIT_ZA, LAST_UNIT_ZC = 6, 22
FIRST_TAKEN = {5: [0], 7: [1], 10: [2], 12: [3], 14: [4], 15: [5, 6, 7, 8]}
UNIT_BEFORE_SCORES = 6
FIRST_OF_GROUP = {3: 0, 7: 1, 8: 2, 9: 3, 10: 4, 23: 5, 24: 6, 25: 7}
FREED_BY = {1: 0, 2: 1, 3: 2, 4: 6, 5: 19, 6: 20, 7: 21, 8: 22}
LAST_UNIT_UPPER = 14
LAST_UNIT_SECOND = 18
ZC_SILU_STEP = 31
STEPS_IN_LAST = (0, 19)
STEPS_OUT_LAST = ((20, 30), (31, 40))


def step_of_end(tile):
    return max(m for m, t in TILE_END.items() if t == tile)


def spread_over(pieces, first, last, steps):
    cost = [QT - BLOCKS[n][2] + STEP_COST if n < NB else TAIL_COST for n in range(first, last + 1)]
    if first == 0:
        cost[0] += FIRST_COST
    done, at = 0, 0
    for n in range(first, last + 1):
        done += cost[n - first]
        want = round(len(pieces) * done / sum(cost))
        while at < want:
            u, _ = pieces[at]
            if len(UNITS_IN) <= u and last == NB and first == 0:
                if n < step_of_end(UNITS_NEXT[u - len(UNITS_IN)][1]) + 1:
                    break
            steps[n].append(pieces[at])
            at += 1
    assert at == len(pieces)


def schedule(last):
    units = UNITS_IN + (UNITS_OUT if last else UNITS_NEXT)
    pieces = [(u, i) for u in range(len(units)) for i in range(PIECES)]
    steps = [[] for _ in range(NB + 1)]
    if last:
        n_in, n_tile = len(UNITS_IN) * PIECES, 2 * SUB * PIECES
        spread_over(pieces[:n_in], *STEPS_IN_LAST, steps)
        spread_over(pieces[n_in:n_in + n_tile], *STEPS_OUT_LAST[0], steps)
        spread_over(pieces[n_in + n_tile:], *STEPS_OUT_LAST[1], steps)
    else:
        spread_over(pieces, 0, NB, steps)
    return units, steps


def layer_program(nc, x, x_blocks, w_blocks, conv_taps_in, w_out, ln_gain, ln_bias, out):
    mix_hi = nc.dram_tensor("mix_hi", [2 * PAIRS, PART, SEQ], F16, kind="Internal").ap()
    mix_lo = nc.dram_tensor("mix_lo", [2 * PAIRS, PART, SEQ], F16, kind="Internal").ap()
    x_rows = x[0].rearrange("(i p) d -> i p d", p=PART)
    out_rows = out[0].rearrange("(i p) d -> i p d", p=PART)
    wo_rows = w_out[0].rearrange("(c p) n -> c p n", p=PART)

    with ExitStack() as ctx:
        def sb(name, shape, dt):
            return ctx.enter_context(nc.sbuf_tensor(name, shape, dt))

        def sem(name):
            return ctx.enter_context(nc.semaphore(name))

        xt_hi = sb("xt_hi", [PART, DCH, SEQ], F16)
        xt_lo = sb("xt_lo", [PART, DCH, SEQ], F16)
        w_raw = sb("w_raw", [PART, 2, DCH, PART], F32)
        w_hi = sb("w_hi", [PART, 4, DCH, PART], F16)
        w_lo = sb("w_lo", [PART, 4, DCH, PART], F16)
        q_hi = sb("q_hi", [PART, SEQ], F16)
        q_lo = sb("q_lo", [PART, SEQ], F16)
        k_hi = sb("k_hi", [PART, SEQ], F16)
        k_lo = sb("k_lo", [PART, SEQ], F16)
        v_hi = sb("v_hi", [PART, NTB, PART], F16)
        v_lo = sb("v_lo", [PART, NTB, PART], F16)
        sp = sb("sp", [PART, 2, 2, QT], F32)
        sp_hi = sb("sp_hi", [PART, 2, 2, QT], F16)
        sp_lo = sb("sp_lo", [PART, 2, 2, QT], F16)
        wt = sb("wt", [PART, 2, QT], F32)
        wt_hi = sb("wt_hi", [PART, 2, 2, QT], F16)
        wt_lo = sb("wt_lo", [PART, 2, 2, QT], F16)
        carry_hi = sb("carry_hi", [PART, QT], F16)
        carry = sb("carry", [PART, QT], F16)
        u_conv = sb("u_conv", [PART, CONV_K - 1 + SEQ], F32)
        b_gate = sb("b_gate", [PART, SEQ], F32)
        z_conv = sb("z_conv", [PART, SEQ], F32)
        z_attn = sb("z_attn", [PART, SEQ], F32)
        y_conv = sb("y_conv", [PART, 2, QT], F32)
        cm_hi = sb("cm_hi", [PART, QT], F16)
        cm_lo = sb("cm_lo", [PART, QT], F16)
        o_gated = sb("o_gated", [PART, QT], F32)
        om_hi = sb("om_hi", [PART, QT], F16)
        om_lo = sb("om_lo", [PART, QT], F16)
        tri = sb("tri", [PART, PART], F16)
        future = sb("future", [PART, PART], F16)
        root_id = sb("root_id", [PART, PART], F16)
        ones = sb("ones", [PART, 32], F16)
        spread = sb("spread", [PART, PART], F16)
        rest_rows = sb("rest_rows", [PART, 1], F32)
        p_bias = sb("p_bias", [PART, 1], F32)
        eps = sb("eps", [PART, 1], F32)
        w_scale = sb("w_scale", [PART, 1], F32)
        taps = sb("taps", [PART, PAIRS, CONV_K], F32)
        given = sb("given", [PART, 8], F32)
        stats = sb("stats", [PART, 2, 12], F32)
        mean_var = sb("mean_var", [PART, 2, 2], F32)
        log_var = sb("log_var", [PART, 2], F32)
        rstd = sb("rstd", [PART, 2], F32)

        arg = [ctx.enter_context(nc.psum_tensor(f"arg{i}", [PART, 2, QT], F32)) for i in range(2)]
        sums = ctx.enter_context(nc.psum_tensor("sums", [PART, QT], F32))
        o_acc = ctx.enter_context(nc.psum_tensor("o_acc", [PART, QT], F32))
        proj = [ctx.enter_context(nc.psum_tensor(f"proj{i}", [PART, QT], F32)) for i in range(2)]

        x_in = [buf[:, h * D_MODEL:(h + 1) * D_MODEL] for buf in (b_gate, z_conv, z_attn) for h in range(2)]
        NX = len(x_in)
        UPPER = SEQ - D_MODEL
        wo_hi, wo_lo = xt_hi[:, :, UPPER:SEQ], xt_lo[:, :, UPPER:SEQ]
        mx_hi, mx_lo = ([xt[:, :, i * QT:(i + 1) * QT] for i in (1, 0)] for xt in (xt_hi, xt_lo))
        rows = [buf[:, h * D_MODEL:(h + 1) * D_MODEL] for h in (1, 0) for buf in (b_gate, z_conv)]
        gain, bias = (w_raw[:, i, :, :].rearrange("p c m -> p (c m)") for i in range(2))
        NR = len(rows)

        consts_done = sem("consts_done")
        rows_done = sem("rows_done")
        taps_loaded = sem("taps_loaded")
        x_loaded = [sem(f"x_loaded{i}") for i in range(NX)]
        xh_done, xl_done = sem("xh_done"), sem("xl_done")
        w_loaded = [sem(f"w_loaded{i}") for i in range(2)]
        first_w_high = sem("first_w_high")
        w_part = sem("w_part")
        w_ready = sem("w_ready")
        unit_done = sem("unit_done")
        proj_free = [sem(f"proj_free{i}") for i in range(2)]
        hi_done = sem("hi_done")
        z_ready = sem("z_ready")
        min_done, exp1_done, ln_done = sem("min_done"), sem("exp1_done"), sem("ln_done")
        sp_done, sph_done, spl_done = sem("sp_done"), sem("sph_done"), sem("spl_done")
        sums_ready, chi_done, carry_done = sem("sums_ready"), sem("chi_done"), sem("carry_done")
        arg_ready = sem("arg_ready")
        wt_done, wth_done, wtl_done = sem("wt_done"), sem("wth_done"), sem("wtl_done")
        pv_done = sem("pv_done")
        o_taken, omh_done, oml_done = sem("o_taken"), sem("omh_done"), sem("oml_done")
        om_stored = sem("om_stored")
        gate_in = sem("gate_in")
        u_done = sem("u_done")
        silu_done = sem("silu_done")
        y_step, gates_done, mixed, cmh_done, cml_done = (sem(n) for n in
                                                         ("y_step", "gates_done", "mixed", "cmh_done", "cml_done"))
        cm_stored = sem("cm_stored")
        wo_loaded = [sem(f"wo_loaded{i}") for i in range(2)]
        woh_done, wol_done = sem("woh_done"), sem("wol_done")
        affine_loaded, gain_scaled = sem("affine_loaded"), sem("gain_scaled")
        mx_loaded = [sem(f"mx_loaded{i}") for i in range(2)]
        row_loaded = [sem(f"row_loaded{i}") for i in range(NR)]
        mx_later = sem("mx_later")
        sub_ready, row_summed = sem("sub_ready"), sem("row_summed")
        stats_done, var_done, log_done, rstd_done = (sem(n) for n in
                                                     ("stats_done", "var_done", "log_done", "rstd_done"))
        norm_step, row_done = sem("norm_step"), sem("row_done")
        row_stored = [sem(f"row_stored{i}") for i in range(NR)]

        block = ctx.enter_context(nc.Block())

        PV_CREDIT, WTL_CREDIT, O_CREDIT, CML_CREDIT = 2, 1, 1, 2
        STORE_CREDIT = 32
        N_CONSTS, N_ROWS = 8 + 3, 10

        units_mid, steps_mid = schedule(False)
        units_last, steps_last = schedule(True)

        def plan(last):
            return (units_last, steps_last) if last else (units_mid, steps_mid)

        def unit_ends(last):
            _, steps = plan(last)
            ends = [[] for _ in range(NB + 1)]
            for n, mine in enumerate(steps):
                ends[n] += [u for u, i in mine if i == PIECES - 1]
            return ends

        def silu_units(last):
            return (LAST_UNIT_ZA, LAST_UNIT_UPPER, LAST_UNIT_ZC) if last else (LAST_UNIT_ZA, LAST_UNIT_ZC)

        def silu_step(u, last):
            return max(end_of(last, u) + 1, ZC_SILU_STEP if u == LAST_UNIT_ZC and not last else 0)

        def early_pieces(n, last):
            units, steps = plan(last)
            most = (len(steps[n]) + 1) // 2
            if any(silu_step(u, last) == n - 1 for u in silu_units(last)):
                most = len(steps[n])
            for k, (u, _) in enumerate(steps[n][:most]):
                if not last and u >= len(UNITS_IN) and step_of_end(units[u][1]) + 1 == n:
                    return k
            return most

        def early_ends(n, last):
            mine = plan(last)[1][n]
            return [u for u, i in mine[:early_pieces(n, last)] if i == PIECES - 1] if n < NB else []

        def late_ends(n, last):
            return [u for u in unit_ends(last)[n] if u not in early_ends(n, last)]

        def end_of(last, unit):
            return next(n for n, us in enumerate(unit_ends(last)) if unit in us)

        def split_steps(last):
            out = [[] for _ in range(NB + 1)]
            for j, unit in FREED_BY.items():
                if not last or j <= 4:
                    out[end_of(last, unit)].append(j)
            return out

        def h_unit(tile):
            return UNITS_IN.index((G_H, tile, 1))

        def conv_events(n, last):
            first = silu_step(LAST_UNIT_ZC, last) + 1
            starts = [first + k for k in range(NQT)]
            if last:
                upper = silu_step(LAST_UNIT_UPPER, last) + 1
                starts = [upper, max(upper + 1, end_of(last, h_unit(1)) + 1), first, first + 1]
            out = []
            for k, at in enumerate(starts):
                if min(at, NB) == n:
                    out.append(("start", k))
                if min(at + 1, NB) == n:
                    out.append(("finish", k))
            return sorted(out, key=lambda e: (e[1], e[0] == "finish"))

        def out_weights_at(n, last):
            if not last:
                return []
            first = end_of(last, LAST_UNIT_UPPER) + 1
            return [c for c in range(DCH) if first + c * 3 // 4 == n]

        def out_units_at(n, last):
            if not last:
                return []
            return [u for u in (late_ends(n - 1, last) if n >= 1 else []) + (early_ends(n, last) if n <= NB else [])
                    if u >= len(UNITS_IN)]

        def rows_at(n, last):
            return [units_last[u][1] for u in out_units_at(n, last) if units_last[u][2] == 1]

        def taken_count(p, u):
            return p * (N_UNITS // 2) + ((N_FIRST + u) // 2 + 1)

        GROUPS = [G_ZA, G_C, G_H, G_B, G_ZC, G_V, G_Q, G_K, G_ZA, G_C]

        def row_of(r):
            return (NQT - 1 - r // SUB) * SUB + r % SUB

        def load_mixed(eng, m):
            t, i = NQT - 1 - m, m % 2
            before = (LAST_UNIT_SECOND + 1, LAST_UNIT_ZC + 1, len(UNITS_IN) + 2 * SUB, len(UNITS_IN) + 4 * SUB)
            eng.wait_ge(unit_done, N_FIRST + N_UNITS * (PAIRS - 1) + before[m])
            if m == 3:
                eng.wait_ge(mx_later, 32)
            stored = STORE_CREDIT + 32 * (NQT * (PAIRS - 1) + m + 1)
            eng.wait_ge(om_stored, stored)
            eng.wait_ge(cm_stored, stored)
            for src, dst in ((mix_hi, mx_hi[i]), (mix_lo, mx_lo[i])):
                eng.dma_start(dst, src.rearrange("c p t -> p c t")[:, :, t * QT:(t + 1) * QT])\
                    .then_inc(mx_loaded[i] if m < 2 else mx_later, 16)

        def load_row(eng, r, i):
            eng.dma_start(rows[i], x_rows[row_of(r)]).then_inc(row_loaded[i], 16)

        def load_group(sp_eng, g_index, slot, group, pair):
            sp_eng.dma_start(w_raw[:, slot, :, :].rearrange("p c m -> p (c m)"), w_blocks[group, pair])\
                .then_inc(w_loaded[slot], 16)

        @block.sync
        def _(eng):
            load_group(eng, 0, 0, G_V, 0)
            for k in range(NX):
                eng.dma_start(x_in[k], x_blocks[NTB - 1 - k]).then_inc(x_loaded[k], 16)
                if k == 0:
                    load_group(eng, 1, 1, G_Q, 0)
            eng.wait_ge(w_ready, 1)
            load_group(eng, 2, 0, G_K, 0)
            eng.dma_start(taps[:, :, :], conv_taps_in).then_inc(taps_loaded, 16)
            for k in range(NX, NTB):
                if k == NX + 2:
                    eng.wait_ge(w_ready, 2)
                    load_group(eng, 3, 1, G_ZA, 0)
                eng.wait_ge(xh_done, k - NX + 1)
                eng.wait_ge(xl_done, k - NX + 1)
                eng.dma_start(x_in[k % NX], x_blocks[NTB - 1 - k]).then_inc(x_loaded[k % NX], 16)
            eng.wait_ge(w_ready, 3)
            load_group(eng, 4, 0, G_C, 0)

            def pair_stores(p, last):
                splits = split_steps(last)
                for n in range(NB + 1):
                    for j in splits[n]:
                        if j + 1 <= (4 if last else 9) and j + 1 >= 2:
                            g = 3 + (j + 1)
                            eng.wait_ge(w_ready, p * 8 + (g - 2 + 1))
                            load_group(eng, g, g % 2, GROUPS[j + 1], p + (1 if j + 1 >= 5 else 0))
                    for what, t in conv_events(n, last):
                        if what == "start":
                            continue
                        eng.wait_ge(cml_done, p * NQT + (t + 1 + CML_CREDIT))
                        t = NQT - 1 - t
                        eng.dma_start(mix_hi[p, :, t * QT:(t + 1) * QT], cm_hi[:, :]).then_inc(cm_stored, 16)
                        eng.dma_start(mix_lo[p, :, t * QT:(t + 1) * QT], cm_lo[:, :]).then_inc(cm_stored, 16)
                    if n - 1 in TILE_END:
                        t = TILE_END[n - 1]
                        k = NQT - 1 - t
                        eng.wait_ge(oml_done, p * NQT + (k + 1))
                        eng.dma_start(mix_hi[p + PAIRS, :, t * QT:(t + 1) * QT], om_hi[:, :]).then_inc(om_stored, 16)
                        eng.dma_start(mix_lo[p + PAIRS, :, t * QT:(t + 1) * QT], om_lo[:, :]).then_inc(om_stored, 16)
                    for c in out_weights_at(n, last):
                        if c == 0:
                            eng.wait_ge(w_ready, 3 + 8 * (PAIRS - 1) + 5)
                            load_out_weights(eng, 0)
                            load_out_weights(eng, 1)
                        if c + 2 < DCH:
                            eng.wait_ge(wol_done, c + 1)
                            load_out_weights(eng, c + 2)
                    if last and ("finish", 1) in conv_events(n, last):
                        eng.wait_ge(cm_stored, STORE_CREDIT + 32 * (NQT * (PAIRS - 1) + 2))
                        load_row(eng, 0, 0)
                        load_row(eng, 1, 1)
                    if last and ("finish", NQT - 1) in conv_events(n, last):
                        eng.wait_ge(cm_stored, STORE_CREDIT + 32 * NQT * PAIRS)
                        load_row(eng, 2, 2)
                        load_row(eng, 3, 3)
                    if DCH - 1 in out_weights_at(n, last):
                        eng.wait_ge(wol_done, DCH)
                        for name, dst in ((ln_gain, gain), (ln_bias, bias)):
                            eng.dma_start(dst, name[0:1, :].broadcast_to([PART, D_MODEL])).then_inc(affine_loaded, 16)
                    for m in range(NQT):
                        finish = next(s for s in range(NB + 1) if ("finish", m) in conv_events(s, last))
                        place_free = end_of(last, LAST_UNIT_SECOND if m == 0 else LAST_UNIT_ZC) + 1
                        if last and n == max(finish, step_of_end(NQT - 1 - m) + 1, place_free):
                            load_mixed(eng, m)
                    for r in rows_at(n - 1, last):
                        store_row(eng, r)

            def load_out_weights(eng, c):
                eng.dma_start(w_raw[:, c % 2, :, :].rearrange("p c m -> p (c m)"), wo_rows[c])\
                    .then_inc(wo_loaded[c % 2], 16)

            def store_row(eng, r):
                eng.wait_ge(row_done, r + 1)
                eng.dma_start(out_rows[row_of(r)], rows[r % NR]).then_inc(row_stored[r % NR], 16)
                if r >= 1 and r - 1 + NR < NTB:
                    eng.wait_ge(row_stored[(r - 1) % NR], 16 * ((r - 1) // NR + 1))
                    load_row(eng, r - 1 + NR, (r - 1) % NR)

            for p in range(PAIRS):
                pair_stores(p, p == PAIRS - 1)

            for r in rows_at(NB, True) + rows_at(NB + 1, True):
                store_row(eng, r)
            for r in range(ROWS_EARLY, NTB):
                store_row(eng, r)
            for i in range(NR):
                eng.wait_ge(row_stored[i], 16 * (NTB // NR))

        @block.tensor
        def _(pe):
            mm = nc.tensor.matmul

            def unit_products(unit):
                group, t, slot = unit
                prods = []
                if group == G_OUT:
                    r, half = t, slot
                    i, tok = r // SUB, slice(r % SUB * PART, (r % SUB + 1) * PART)
                    for c in range(DCH):
                        for a, b in ((mx_hi, wo_hi), (mx_hi, wo_lo), (mx_lo, wo_hi)):
                            prods.append((slice(0, QT), a[i][:, c, tok], b[:, c, half * QT:(half + 1) * QT],
                                          c == 0 and a is mx_hi and b is wo_hi,
                                          c == DCH - 1 and a is mx_lo))
                elif group == G_V:
                    for s in reversed(range(SUB)):
                        tok = slice(t * QT + s * PART, t * QT + (s + 1) * PART)
                        for d in range(DCH):
                            for a, b in ((xt_hi, w_hi), (xt_hi, w_lo), (xt_lo, w_hi)):
                                prods.append((slice(s * PART, (s + 1) * PART), a[:, d, tok], b[:, slot, d, :],
                                              d == 0 and a is xt_hi and b is w_hi,
                                              d == DCH - 1 and a is xt_lo))
                else:
                    tok = slice(t * QT, (t + 1) * QT)
                    for d in range(DCH):
                        for a, b in ((w_hi, xt_hi), (w_hi, xt_lo), (w_lo, xt_hi)):
                            prods.append((slice(0, QT), a[:, slot, d, :], b[:, d, tok],
                                          d == 0 and a is w_hi and b is xt_hi,
                                          d == DCH - 1 and a is w_lo))
                return prods

            def unit_piece(p, index, unit, piece, wait_weights):
                prods = unit_products(unit)
                size = len(prods) // PIECES
                bank = (N_FIRST + index) % 2
                if piece == 0:
                    if wait_weights is not None:
                        pe.wait_ge(w_ready, wait_weights)
                    if unit[0] == G_OUT and unit[2] == 0 and unit[1] % SUB == 0:
                        pe.wait_ge(wol_done, DCH)
                        pe.wait_ge(mx_loaded[unit[1] // SUB], 32)
                    uses = (N_FIRST + index) // 2
                    if index >= 0 or uses > 0:
                        pe.wait_ge(proj_free[bank], p * (N_UNITS // 2) + uses)
                for cols, lhs, rhs, start, stop in prods[piece * size:(piece + 1) * size]:
                    last = mm(proj[bank][:, cols], lhs, rhs, start=start, stop=stop)
                if piece == PIECES - 1:
                    last.then_inc(unit_done, 1)

            def pair_products(p, last, first_scores=False):
                units, steps = plan(last)

                def pieces(todo):
                    for u, i in todo:
                        j = None if units[u][0] == G_OUT else FIRST_OF_GROUP.get(u)
                        weights = None if j is None else p * 8 + (3 + j + 1)
                        unit_piece(p, u, units[u], i, weights)

                def scores(n):
                    t, b, c0 = BLOCKS[n % NB]
                    if n >= 2:
                        pe.wait_ge(wt_done, p * NB + (n - 2 + 1))
                    if t == NQT - 1 and b % SUB == SUB - 1:
                        for bank in range(2):
                            units_before = 3 * (NQT - b // SUB) + N_UNITS * (n // NB)
                            pe.wait_ge(proj_free[bank], p * (N_UNITS // 2) + (units_before + 1 - bank) // 2)
                    keys = slice(b * PART, (b + 1) * PART)
                    cols = slice(t * QT + c0, (t + 1) * QT)
                    diagonal = b >= SUB * t
                    for i, (a, c) in enumerate(((k_hi, q_hi), (k_hi, q_lo), (k_lo, q_hi))):
                        for h in range(2):
                            rows_h = slice(h * HEAD_DIM, (h + 1) * HEAD_DIM)
                            last_mm = mm(arg[n % 2][:, h, c0:QT], a[rows_h, keys], c[rows_h, cols],
                                         start=(i == 0), stop=(i == 2), skip_group_check=True)
                    if diagonal:
                        for h in range(2):
                            last_mm = mm(arg[n % 2][:, h, c0:c0 + PART], root_id[:, :], future[:, :],
                                         start=False, stop=True, skip_group_check=True)
                    last_mm.then_inc(z_ready, 1)

                def carried(n):
                    t, b, c0 = BLOCKS[n]
                    if b == SUB * (t + 1) - 1:
                        return
                    pe.wait_ge(carry_done, p * SUMS + SUMS_BEFORE[n])
                    c1 = BLOCKS[n - 1][2]
                    for h in range(2):
                        rows_h = slice(h * HEAD_DIM, (h + 1) * HEAD_DIM)
                        mm(arg[n % 2][:, h, c1:QT], spread[rows_h, :], carry[rows_h, c1:QT],
                           start=False, stop=True, skip_group_check=True)

                def sums_within(n):
                    t, b, c0 = BLOCKS[n]
                    pe.wait_ge(spl_done, p * NB + (n + 1))
                    carried(n)
                    first = b == SUB * (t + 1) - 1
                    if b > 0:
                        for h in range(2):
                            for i, part in enumerate((sp_hi, sp_lo)):
                                quadrant = slice((2 * h + i) * 32, (2 * h + i + 1) * 32)
                                last_mm = mm(sums[quadrant, c0:QT], ones[:, :], part[:, n % 2, h, c0:QT],
                                             start=first, stop=True, skip_group_check=True)
                        last_mm.then_inc(sums_ready, 1)
                    for part in (sp_hi, sp_lo):
                        for h in range(2):
                            last_mm = mm(arg[n % 2][:, h, c0:QT], tri[:, :], part[:, n % 2, h, c0:QT],
                                         start=False, stop=True, skip_group_check=True)
                    last_mm.then_inc(arg_ready, 1)

                def values(n):
                    t, b, c0 = BLOCKS[n]
                    pe.wait_ge(wtl_done, p * NB + (n + 1 + WTL_CREDIT))
                    first = b == SUB * (t + 1) - 1
                    if first:
                        pe.wait_ge(o_taken, p * NQT + (NQT - 1 - t + O_CREDIT))
                    for i, (a, c) in enumerate(((v_hi, wt_hi), (v_hi, wt_lo), (v_lo, wt_hi))):
                        for h in range(2):
                            cols_h = slice(h * HEAD_DIM, (h + 1) * HEAD_DIM)
                            last_mm = mm(o_acc[cols_h, c0:QT], a[:, b, cols_h], c[:, n % 2, h, c0:QT],
                                         start=(first and i == 0), stop=(i == 2), skip_group_check=True)
                    last_mm.then_inc(pv_done, 1)

                if first_scores:
                    scores(0)
                    scores(1)
                    return
                for n in range(NB):
                    early = early_pieces(n, last)
                    sums_within(n)
                    pieces(steps[n][:early])
                    if not last or n + 2 < NB:
                        scores(n + 2)
                    if n >= 1:
                        values(n - 1)
                    pieces(steps[n][early:])
                values(NB - 1)
                pieces(steps[NB])

            first_v = unit_products(UNITS_FIRST[0])
            pe.wait_ge(w_ready, 1)
            for k in range(SUB):
                pe.wait_ge(xl_done, k + 1)
                pe.wait_ge(xh_done, k + 1)
                for cols, lhs, rhs, start, stop in first_v[k * 3 * DCH:(k + 1) * 3 * DCH]:
                    first_mm = mm(proj[0][:, cols], lhs, rhs, start=start, stop=stop)
            first_mm.then_inc(unit_done, 1)
            for i, unit in enumerate(UNITS_FIRST):
                if i == 0:
                    continue
                if i % 3 == 0:
                    pe.wait_ge(xl_done, (i // 3 + 1) * SUB)
                    pe.wait_ge(xh_done, (i // 3 + 1) * SUB)
                for piece in range(PIECES):
                    unit_piece(0, i - N_FIRST, unit, piece, i + 1 if i < 3 else None)
                if i == UNIT_BEFORE_SCORES:
                    pe.wait_ge(consts_done, N_CONSTS)
                    pe.wait_ge(rows_done, N_ROWS)
                    pair_products(0, False, first_scores=True)
            pe.wait_ge(xl_done, NTB)
            pe.wait_ge(xh_done, NTB)

            with pe.Fori(0, PAIRS - 1) as p:
                pair_products(p, False)
            pair_products(PAIRS - 1, True)

            with pe.Fori(0, 2) as tile:
                pe.wait_ge(mx_later, tile * 32 + 32)
                for s in range(SUB):
                    pe.wait_ge(row_summed, tile * (2 * SUB) + 2 * (s - 2 + 1 + 2))
                    for half in range(2):
                        for c in range(DCH):
                            for m, (a, b) in enumerate(((xt_hi, wo_hi), (xt_hi, wo_lo), (xt_lo, wo_hi))):
                                last = mm(arg[s % 2][:, half, :], a[:, c, bass.ds(tile * -QT + (QT + s * PART), PART)],
                                          b[:, c, half * QT:(half + 1) * QT],
                                          start=(c == 0 and m == 0), stop=(c == DCH - 1 and m == 2))
                        last.then_inc(sub_ready, 1)

        def high_place(unit):
            group, t, _ = unit
            tok = slice(t * QT, (t + 1) * QT)
            if group == G_V:
                return (v_hi[:, t * SUB:(t + 1) * SUB, :].rearrange("p s c -> p (s c)"),
                        v_lo[:, t * SUB:(t + 1) * SUB, :].rearrange("p s c -> p (s c)"))
            return (q_hi[:, tok], q_lo[:, tok]) if group == G_Q else (k_hi[:, tok], k_lo[:, tok])

        def first_hi(act, i):
            act.wait_ge(unit_done, i + 1)
            nc.scalar.activation(high_place(UNITS_FIRST[i])[0], proj[i % 2][:, :], ACT.Copy, scale=PROJ_SCALE)\
                .then_inc(hi_done, 1)

        def hi_count(u):
            return u + 1 if u < 3 else 3 + (u - len(UNITS_IN)) + 1

        def take_unit(act, p, u, unit):
            group, t, _ = unit
            bank = (N_FIRST + u) % 2
            tok = slice(t * QT, (t + 1) * QT)
            if group in (G_H, G_OUT):
                return
            act.wait_ge(unit_done, p * N_UNITS + (N_FIRST + u + 1))
            if group in (G_Q, G_K, G_V):
                nc.scalar.activation(high_place(unit)[0], proj[bank][:, :], ACT.Copy, scale=PROJ_SCALE)\
                    .then_inc(hi_done, 1)
                return
            dst = {G_ZA: z_attn[:, tok], G_B: b_gate[:, tok], G_ZC: z_conv[:, tok],
                   G_C: u_conv[:, CONV_K - 1 + t * QT:CONV_K - 1 + (t + 1) * QT]}[group]
            nc.scalar.activation(dst, proj[bank][:, :], ACT.Copy, scale=PROJ_SCALE).then_inc(proj_free[bank], 1)

        def gate_silu(act, p, u, unit, last):
            group = unit[0]
            bank = (N_FIRST + u) % 2
            halves = last and group == G_ZC
            gate = z_attn if group == G_ZA else z_conv
            part = slice(0, SEQ) if not halves else slice(UPPER, SEQ) if u == LAST_UNIT_UPPER else slice(0, UPPER)
            for bk, back in ((bank, 0), (1 - bank, 1)):
                act.wait_ge(proj_free[bk], taken_count(p, u - back))
            nc.scalar.activation(gate[:, part], gate[:, part], ACT.Silu).then_inc(silu_done, 1)
            nc.scalar.preload_act_table_set(TABLES)

        @block.scalar
        def _(act):
            act.wait_ge(consts_done, N_CONSTS)
            nc.scalar.preload_act_table_set(TABLES)
            def deviation(act, i, count):
                act.wait_ge(var_done, count)
                nc.scalar.activation(log_var[:, i % 2:i % 2 + 1], mean_var[:, i % 2, 1:2], ACT.Ln,
                                     bias=eps[:, :], scale=1.0 / W_SCALE ** 2).then_inc(log_done, 1)
                act.wait_ge(log_done, count)
                nc.scalar.activation(rstd[:, i % 2:i % 2 + 1], log_var[:, i % 2:i % 2 + 1], ACT.Exp,
                                     scale=-0.5).then_inc(rstd_done, 1)

            def pair_activations(p, last, first_blocks=False):
                units, _ = plan(last)

                def softplus_terms(n):
                    e = sp[:, n % 2, :, BLOCKS[n % NB][2]:QT]
                    act.wait_ge(min_done, p * NB + (n + 1))
                    nc.scalar.activation(e, e, ACT.Exp).then_inc(exp1_done, 1)
                    act.wait_ge(exp1_done, p * NB + (n + 1))
                    nc.scalar.activation(e, e, ACT.Ln, bias=1.0).then_inc(ln_done, 1)

                def softplus_high(n):
                    c0 = BLOCKS[n % NB][2]
                    act.wait_ge(sp_done, p * NB + (n + 1))
                    nc.scalar.activation(sp_hi[:, n % 2, :, c0:QT], sp[:, n % 2, :, c0:QT], ACT.Copy)\
                        .then_inc(sph_done, 1)

                if first_blocks:
                    for n in range(2):
                        softplus_terms(n)
                    softplus_high(0)
                    return
                for n in range(NB + 1):
                    more = n < NB and (not last or n + 2 < NB)
                    if n < NB:
                        c0 = BLOCKS[n][2]
                        act.wait_ge(arg_ready, p * NB + (n + 1))
                        act.wait_ge(wtl_done, p * NB + (n + WTL_CREDIT))
                        nc.scalar.activation(wt[:, :, c0:QT], arg[n % 2][:, :, c0:QT], ACT.Exp,
                                             bias=p_bias[:, :], scale=1.0 / ROOT).then_inc(wt_done, 1)
                        if not last or n + 1 < NB:
                            softplus_high(n + 1)
                        act.wait_ge(wt_done, p * NB + (n + 1))
                        act.wait_ge(pv_done, p * NB + (n - 2 + 1 + PV_CREDIT))
                        nc.scalar.activation(wt_hi[:, n % 2, :, c0:QT], wt[:, :, c0:QT], ACT.Copy)\
                            .then_inc(wth_done, 1)
                    for u in early_ends(n, last):
                        take_unit(act, p, u, units[u])
                    for u in silu_units(last):
                        if silu_step(u, last) == n:
                            gate_silu(act, p, u, units[u], last)
                    if more:
                        softplus_terms(n + 2)
                    for u in late_ends(n, last):
                        take_unit(act, p, u, units[u])
                    for c in out_weights_at(n, last):
                        act.wait_ge(wo_loaded[c % 2], 16 * (c // 2 + 1))
                        if c == 0:
                            act.wait_ge(unit_done, N_FIRST + N_UNITS * (PAIRS - 1) + LAST_UNIT_UPPER + 1)
                        nc.scalar.activation(wo_hi[:, c, :], w_raw[:, c % 2, :, :].rearrange("p c m -> p (c m)"),
                                             ACT.Copy, scale=W_SCALE).then_inc(woh_done, 1)
                    for r in rows_at(n, last):
                        deviation(act, r % NR, r + 1)

            act.wait_ge(w_loaded[0], 16)
            nc.scalar.activation(w_hi[:, 0, :, :], w_raw[:, 0, :, :], ACT.Copy, scale=W_SCALE)\
                .then_inc(first_w_high, 1)
            for k in range(NTB):
                act.wait_ge(x_loaded[k % NX], 16 * (k // NX + 1))
                blk = NTB - 1 - k
                nc.scalar.activation(xt_hi[:, :, blk * PART:(blk + 1) * PART],
                                     x_in[k % NX].rearrange("p (c t) -> p c t", t=PART),
                                     ACT.Copy, scale=X_SCALE).then_inc(xh_done, 1)
                for i in FIRST_TAKEN.get(k, []):
                    first_hi(act, i)
                    if i == UNIT_BEFORE_SCORES:
                        pair_activations(0, False, first_blocks=True)

            with act.Fori(0, PAIRS - 1) as p:
                pair_activations(p, False)
            pair_activations(PAIRS - 1, True)

            for r in rows_at(NB + 1, True):
                deviation(act, r % NR, r + 1)
            with act.Fori(0, 2) as tile:
                for s in range(SUB):
                    deviation(act, s, tile * SUB + (ROWS_EARLY + s + 1))

        def first_low(dve, i):
            dve.wait_ge(hi_done, i + 1)
            hi, lo = high_place(UNITS_FIRST[i])
            nc.vector.scalar_tensor_tensor(out=lo, in0=proj[i % 2][:, :], scalar=PROJ_SCALE, in1=hi, op0=ALU.mult,
                                           op1=ALU.subtract).then_inc(proj_free[i % 2], 1)

        @block.vector
        def _(dve):
            stt = nc.vector.scalar_tensor_tensor

            nc.vector.memset(spread[:, :], 0.0).then_inc(rows_done, 1)
            nc.vector.memset(rest_rows[:, :], 0.0).then_inc(rows_done, 1)
            dve.wait_ge(rows_done, 2)
            for h in range(2):
                top = h * HEAD_DIM
                nc.vector.memset(spread[top:top + 2, :], -ROOT).then_inc(rows_done, 1)
                nc.vector.memset(spread[top + 32:top + 33, :], -ROOT).then_inc(rows_done, 1)
                nc.vector.memset(rest_rows[top:top + 2, :], 1.0).then_inc(rows_done, 1)
            dve.wait_ge(rows_done, 8)
            for h in range(2):
                nc.vector.memset(rest_rows[h * HEAD_DIM:h * HEAD_DIM + 1, :], 0.0).then_inc(rows_done, 1)
            dve.wait_ge(consts_done, N_CONSTS)
            dve.wait_ge(rows_done, N_ROWS)
            def half_statistics(i, half):
                nc.vector.bn_stats(stats[:, i % 2, 6 * half:6 * half + 6], rows[i][:, half * QT:(half + 1) * QT])\
                    .then_inc(stats_done, 1)

            def mean_and_variance(i, count):
                dve.wait_ge(stats_done, count(2))
                nc.vector.memset(given[:, 0:1], 0.0)
                nc.vector.bn_aggr(mean_var[:, i % 2, :], stats[:, i % 2, :]).then_inc(var_done, 1)

            def normalise(i, before):
                dve.wait_ge(var_done, before(1) + 1)
                stt(out=rows[i], in0=rows[i], scalar=mean_var[:, i % 2, 0:1], in1=gain,
                    op0=ALU.subtract, op1=ALU.mult).then_inc(norm_step, 1)
                dve.wait_ge(norm_step, before(1) + 1)
                dve.wait_ge(rstd_done, before(1) + 1)
                stt(out=rows[i], in0=rows[i], scalar=rstd[:, i % 2:i % 2 + 1], in1=bias,
                    op0=ALU.mult, op1=ALU.add).then_inc(row_done, 1)

            def pair_vectors(p, last, first_blocks=False):
                units, _ = plan(last)

                def clamp(n):
                    c0 = BLOCKS[n % NB][2]
                    dve.wait_ge(z_ready, p * NB + (n + 1))
                    nc.vector.tensor_scalar(sp[:, n % 2, :, c0:QT], arg[n % 2][:, :, c0:QT], 1.0 / ROOT, EXP_CLAMP,
                                            ALU.mult, ALU.min).then_inc(min_done, 1)

                def softplus_guard(n):
                    c0 = BLOCKS[n % NB][2]
                    dve.wait_ge(ln_done, p * NB + (n + 1))
                    stt(out=sp[:, n % 2, :, c0:QT], in0=arg[n % 2][:, :, c0:QT], scalar=1.0 / ROOT,
                        in1=sp[:, n % 2, :, c0:QT], op0=ALU.mult, op1=ALU.max).then_inc(sp_done, 1)

                def softplus_low(n):
                    c0 = BLOCKS[n % NB][2]
                    dve.wait_ge(sph_done, p * NB + (n + 1))
                    nc.vector.tensor_tensor(sp_lo[:, n % 2, :, c0:QT], sp[:, n % 2, :, c0:QT], sp_hi[:, n % 2, :, c0:QT],
                                            ALU.subtract).then_inc(spl_done, 1)

                def split_carry(n):
                    _, b, c0 = BLOCKS[n]
                    if b == 0:
                        return
                    dve.wait_ge(sums_ready, p * SUMS + (SUMS_BEFORE[n] + 1))
                    nc.vector.tensor_scalar(carry_hi[:, c0:QT], sums[:, c0:QT], CUT, rest_rows[:, :],
                                            ALU.min, ALU.mult).then_inc(chi_done, 1)
                    dve.wait_ge(chi_done, p * SUMS + (SUMS_BEFORE[n] + 1))
                    stt(out=carry[:, c0:QT], in0=sums[:, c0:QT], scalar=CUT, in1=carry_hi[:, c0:QT],
                        op0=ALU.min, op1=ALU.subtract).then_inc(carry_done, 1)

                def take(u):
                    group, t, _ = units[u]
                    bank = (N_FIRST + u) % 2
                    if group == G_H:
                        dve.wait_ge(unit_done, p * N_UNITS + (N_FIRST + u + 1))
                        dve.wait_ge(proj_free[1 - bank], taken_count(p, u - 1))
                        at = u_conv[:, CONV_K - 1 + t * QT:CONV_K - 1 + (t + 1) * QT]
                        stt(out=at, in0=proj[bank][:, :], scalar=PROJ_SCALE, in1=at, op0=ALU.mult, op1=ALU.mult)\
                            .then_inc(proj_free[bank], 1)
                    elif group == G_OUT:
                        r, half = units[u][1:]
                        cols = slice(half * QT, (half + 1) * QT)
                        dve.wait_ge(unit_done, p * N_UNITS + (N_FIRST + u + 1))
                        if half == 0:
                            dve.wait_ge(row_loaded[r % NR], 16 * (r // NR + 1))
                        stt(out=rows[r % NR][:, cols], in0=rows[r % NR][:, cols], scalar=ALPHA * W_SCALE,
                            in1=proj[bank][:, :], op0=ALU.mult, op1=ALU.add).then_inc(proj_free[bank], 1)
                        dve.wait_ge(proj_free[bank], taken_count(p, u))
                        half_statistics(r % NR, half)
                        if half == 1:
                            mean_and_variance(r % NR, lambda per: per * (r + 1))
                    elif group in (G_Q, G_K, G_V):
                        dve.wait_ge(hi_done, p * 12 + (9 + hi_count(u)))
                        hi, lo = high_place(units[u])
                        stt(out=lo, in0=proj[bank][:, :], scalar=PROJ_SCALE, in1=hi, op0=ALU.mult,
                            op1=ALU.subtract).then_inc(proj_free[bank], 1)

                def conv_taps(t):
                    near = h_unit(max(0, NQT - 2 - t))
                    dve.wait_ge(proj_free[(N_FIRST + near) % 2], taken_count(p, near))
                    dve.wait_ge(cml_done, p * NQT + (t - 1 + CML_CREDIT))
                    y = y_conv[:, t % 2, :]
                    base = (NQT - 1 - t) * QT
                    nc.vector.tensor_scalar(y, u_conv[:, base + 2:base + 2 + QT], taps[:, bass.ds(p, 1), 2],
                                            None, ALU.mult).then_inc(y_step, 1)
                    for j in (1, 0):
                        dve.wait_ge(y_step, p * (3 * NQT) + (3 * t + 2 - j))
                        stt(out=y, in0=u_conv[:, base + j:base + j + QT], scalar=taps[:, bass.ds(p, 1), j],
                            in1=y, op0=ALU.mult, op1=ALU.add).then_inc(y_step, 1)

                def conv_high(t):
                    dve.wait_ge(mixed, p * NQT + (t + 1))
                    dve.wait_ge(cm_stored, p * (32 * NQT) + (32 * t + STORE_CREDIT))
                    nc.vector.tensor_copy(cm_hi[:, :], y_conv[:, t % 2, :]).then_inc(cmh_done, 1)

                def take_output(t):
                    k = NQT - 1 - t
                    n = next(m for m, tt in TILE_END.items() if tt == t)
                    dve.wait_ge(pv_done, p * NB + (n + 1 + PV_CREDIT))
                    if k == 0:
                        dve.wait_ge(silu_done, p * 2 + 1)
                    dve.wait_ge(om_stored, p * (32 * NQT) + (32 * k + STORE_CREDIT))
                    stt(out=o_gated[:, :], in0=o_acc[:, :], scalar=1.0 / P_SCALE,
                        in1=z_attn[:, t * QT:(t + 1) * QT], op0=ALU.mult, op1=ALU.mult).then_inc(o_taken, 1)
                    dve.wait_ge(o_taken, p * NQT + (k + 1 + O_CREDIT))
                    nc.vector.tensor_copy(om_hi[:, :], o_gated[:, :]).then_inc(omh_done, 1)

                if first_blocks:
                    for step in (clamp, softplus_guard):
                        for n in range(2):
                            step(n)
                    softplus_low(0)
                    return
                for n in range(NB + 1):
                    more = n < NB and (not last or n + 2 < NB)
                    if n < NB:
                        split_carry(n)
                    if n < NB and (not last or n + 1 < NB):
                        softplus_low(n + 1)
                    if more:
                        clamp(n + 2)
                    for u in early_ends(n, last):
                        if units[u][0] != G_OUT:
                            take(u)
                    for u in out_units_at(n, last):
                        take(u)
                    if n - 1 in TILE_END:
                        take_output(TILE_END[n - 1])
                    for what, t in conv_events(n, last):
                        (conv_taps if what == "start" else conv_high)(t)
                    for c in out_weights_at(n, last):
                        dve.wait_ge(woh_done, c + 1)
                        stt(out=wo_lo[:, c, :], in0=w_raw[:, c % 2, :, :].rearrange("p c m -> p (c m)"),
                            scalar=W_SCALE, in1=wo_hi[:, c, :], op0=ALU.mult, op1=ALU.subtract).then_inc(wol_done, 1)
                    if 0 in rows_at(n - 1, last):
                        dve.wait_ge(affine_loaded, 32)
                        nc.vector.tensor_scalar(gain, gain, 1.0 / W_SCALE, None, ALU.mult).then_inc(gain_scaled, 1)
                        dve.wait_ge(gain_scaled, 1)
                    for r in rows_at(n - 1, last):
                        normalise(r % NR, lambda per, r=r: per * r)
                    if more:
                        softplus_guard(n + 2)
                    for u in late_ends(n, last):
                        if units[u][0] != G_OUT:
                            take(u)
                for u in out_units_at(NB + 1, last):
                    take(u)
                for r in rows_at(NB, last) + rows_at(NB + 1, last):
                    normalise(r % NR, lambda per, r=r: per * r)

            dve.wait_ge(first_w_high, 1)
            stt(out=w_lo[:, 0, :, :], in0=w_raw[:, 0, :, :], scalar=W_SCALE, in1=w_hi[:, 0, :, :],
                op0=ALU.mult, op1=ALU.subtract).then_inc(w_ready, 1)
            for k in range(NTB):
                dve.wait_ge(xh_done, k + 1)
                blk = NTB - 1 - k
                cols = slice(blk * PART, (blk + 1) * PART)
                stt(out=xt_lo[:, :, cols], in0=x_in[k % NX].rearrange("p (c t) -> p c t", t=PART),
                    scalar=X_SCALE, in1=xt_hi[:, :, cols], op0=ALU.mult, op1=ALU.subtract).then_inc(xl_done, 1)
                for i in FIRST_TAKEN.get(k, []):
                    first_low(dve, i)
                    if i == UNIT_BEFORE_SCORES:
                        pair_vectors(0, False, first_blocks=True)

            dve.wait_ge(taps_loaded, 16)
            with dve.Fori(0, PAIRS - 1) as p:
                pair_vectors(p, False)
            pair_vectors(PAIRS - 1, True)

            with dve.Fori(0, 2) as tile:
                for s in range(SUB):
                    dve.wait_ge(row_loaded[s], tile * 16 + 16 * (ROWS_EARLY // NR + 1))
                    for half in range(2):
                        cols = slice(half * QT, (half + 1) * QT)
                        dve.wait_ge(sub_ready, tile * (2 * SUB) + (2 * s + half + 1))
                        stt(out=rows[s][:, cols], in0=rows[s][:, cols], scalar=ALPHA * W_SCALE,
                            in1=arg[s % 2][:, half, :], op0=ALU.mult, op1=ALU.add).then_inc(row_summed, 1)
                        dve.wait_ge(row_summed, tile * (2 * SUB) + (2 * s + half + 1 + 4))
                        half_statistics(s, half)
                    mean_and_variance(s, lambda per: tile * (SUB * per) + per * (ROWS_EARLY + s + 1))
                    normalise(s, lambda per: tile * (SUB * per) + per * (ROWS_EARLY + s))

        @block.gpsimd
        def _(pool):
            below = dict(pattern=[[-1, PART]], base=0, channel_multiplier=1)
            credits = [(pv_done, PV_CREDIT), (wtl_done, WTL_CREDIT), (o_taken, O_CREDIT),
                       (cml_done, CML_CREDIT), (om_stored, STORE_CREDIT), (cm_stored, STORE_CREDIT), (row_summed, 4)]
            for i, (what, n) in enumerate(credits):
                nc.gpsimd.memset(given[:, i:i + 1], 0.0).then_inc(what, n)
            fills = [(tri[:, :], -ROOT), (future[:, :], -CUT), (root_id[:, :], 0.0),
                     (ones[:, :], 1.0), (p_bias[:, :], math.log(P_SCALE)),
                     (eps[:, :], LN_EPS), (w_scale[:, :], W_SCALE), (u_conv[:, 0:CONV_K - 1], 0.0)]
            for dst, value in fills:
                nc.gpsimd.memset(dst, value).then_inc(consts_done, 1)
            pool.wait_ge(consts_done, len(fills))
            for dst in (tri, future):
                nc.gpsimd.affine_select(out=dst[:, :], in_=dst[:, :], compare_op=ALU.is_ge, fill=0.0, **below)\
                    .then_inc(consts_done, 1)
            for dst, value in ((root_id, ROOT),):
                nc.gpsimd.affine_select(out=dst[:, :], in_=dst[:, :], compare_op=ALU.not_equal, fill=value, **below)\
                    .then_inc(consts_done, 1)

            def split_weights(slot, raw, loaded, ready_before, first=False):
                pool.wait_ge(w_loaded[raw], loaded)
                flat = lambda a: a.rearrange("p c m -> p (c m)")
                w = flat(w_raw[:, raw, :, :])
                hi, lo = flat(w_hi[:, slot, :, :]), flat(w_lo[:, slot, :, :])
                nc.gpsimd.tensor_tensor(hi, w, w_scale[:, 0:1].broadcast_to([PART, D_MODEL]), ALU.mult)\
                    .then_inc(w_part, 1)
                nc.gpsimd.tensor_scalar(w, w, W_SCALE, 1.0, ALU.mult, ALU.mult).then_inc(w_part, 1)
                pool.wait_ge(w_part, ready_before)
                if first:
                    pool.wait_ge(w_ready, 1)
                nc.gpsimd.tensor_tensor(lo, w, hi, ALU.subtract).then_inc(w_ready, 1)

            for g in range(1, 4):
                split_weights(g, g % 2, 16 * (g // 2 + 1), 2 * g, first=(g == 1))

            def pair_pool(p, last):
                splits = split_steps(last)
                for n in range(NB + 1):
                    if n < NB:
                        c0 = BLOCKS[n][2]
                        pool.wait_ge(wth_done, p * NB + (n + 1))
                        nc.gpsimd.tensor_tensor(wt_lo[:, n % 2, :, c0:QT], wt[:, :, c0:QT],
                                                wt_hi[:, n % 2, :, c0:QT], ALU.subtract).then_inc(wtl_done, 1)
                    for j in splits[n]:
                        g = 3 + j
                        unit = FREED_BY[j]
                        pool.wait_ge(unit_done, p * N_UNITS + (N_FIRST + unit + 1))
                        split_weights(g % 4, g % 2, p * 64 + 16 * (g // 2 + 1), p * 16 + 2 * g)
                    for what, t in conv_events(n, last):
                        tok = slice((NQT - 1 - t) * QT, (NQT - t) * QT)
                        if what == "start":
                            pool.wait_ge(silu_done, p * 2 + (3 if last and t >= 2 else 2))
                            nc.gpsimd.tensor_tensor(b_gate[:, tok], b_gate[:, tok], z_conv[:, tok], ALU.mult)\
                                .then_inc(gates_done, 1)
                            pool.wait_ge(gates_done, p * NQT + (t + 1))
                            pool.wait_ge(y_step, p * (3 * NQT) + 3 * (t + 1))
                            nc.gpsimd.tensor_tensor(y_conv[:, t % 2, :], y_conv[:, t % 2, :], b_gate[:, tok], ALU.mult)\
                                .then_inc(mixed, 1)
                        else:
                            pool.wait_ge(cmh_done, p * NQT + (t + 1))
                            nc.gpsimd.tensor_tensor(cm_lo[:, :], y_conv[:, t % 2, :], cm_hi[:, :], ALU.subtract)\
                                .then_inc(cml_done, 1)
                    if n - 1 in TILE_END:
                        k = NQT - 1 - TILE_END[n - 1]
                        pool.wait_ge(omh_done, p * NQT + (k + 1))
                        nc.gpsimd.tensor_tensor(om_lo[:, :], o_gated[:, :], om_hi[:, :], ALU.subtract)\
                            .then_inc(oml_done, 1)

            with pool.Fori(0, PAIRS - 1) as p:
                pair_pool(p, False)
            pair_pool(PAIRS - 1, True)


_OUT = ((1, SEQ, D_MODEL), "float32")


def kernel(**inputs):
    import numpy as _np
    import concourse.bacc as _bacc
    from concourse import mybir as _mybir
    from concourse.bass_utils import run_bass_kernel_spmd as _run

    nc = _bacc.Bacc("TRN2", target_bir_lowering=False, num_devices=1)
    arrays, args = {}, []
    laid_out = {
        "x": inputs["x"],
        "x_blocks": inputs["x"][0].reshape(NTB, PART, DCH, PART).transpose(0, 3, 2, 1).reshape(NTB, PART, D_MODEL),
        "w_blocks": inputs["w_in"][0].reshape(DCH, PART, 8, PAIRS, PART).transpose(2, 3, 1, 0, 4)
                    .reshape(8, PAIRS, PART, D_MODEL),
        "conv_taps": inputs["conv_w"][0].reshape(CONV_K, PAIRS, PART).transpose(2, 1, 0),
        "w_out": inputs["w_out"], "ln_gain": inputs["ln_gain"], "ln_bias": inputs["ln_bias"],
    }
    for name, laid in laid_out.items():
        a = _np.ascontiguousarray(laid)
        arrays[f"in_{name}_dram"] = a
        args.append(nc.dram_tensor(f"in_{name}_dram", a.shape, _mybir.dt.from_np(a.dtype), kind="ExternalInput").ap())
    shape, dtype = _OUT
    args.append(nc.dram_tensor("out_0_dram", shape, _mybir.dt.from_np(_np.dtype(dtype)), kind="ExternalOutput").ap())
    layer_program(nc, *args)
    r = _run(nc, [arrays], core_ids=[0])
    return r.results[0]["out_0_dram"]
```
